# Optimizing a Trainium2 kernel written in Bass

```python
import jax, jax.numpy as jnp
from jax import lax
import numpy as np

D_MODEL = 2048
BATCH = 1
SEQ = 1024
DEPTH = 1

CHUNK = 64
LEFT_CHUNKS = 8
N_BAND = LEFT_CHUNKS + 1
HEAD_DIM = 128
D_MIX = D_MODEL
D_A = D_MIX // 2
D_B = D_MIX - D_A
H_A = D_A // HEAD_DIM
H_B = D_B // HEAD_DIM
REL_CLIP = 128
H_IDX = 8
D_IDX = 64
TOPK_MAX = 256
Q_BLOCK = 128
D_PLE = 256
ROPE_THETA = 10000.0
LN_EPS = 1e-5
NEG = -1e30
ALPHA = (2.0 * DEPTH) ** 0.25
BETA = (8.0 * DEPTH) ** -0.25
SPLIT_SIZES = (D_A, D_A, D_A, D_A, D_B, HEAD_DIM, HEAD_DIM, D_B, H_IDX * D_IDX, D_IDX, H_IDX)
V_PARTS = (2, 6)
D_IN = sum(SPLIT_SIZES)
SPLIT_IDX = tuple(int(v) for v in np.cumsum(SPLIT_SIZES)[:-1])

kernel_name = 'hybrid_chunk_relpos_dsa_deepnorm'

def layer_norm(x, g, b):
    xf = x.astype(jnp.float32)
    mu = jnp.mean(xf, -1, keepdims=True)
    var = jnp.mean(jnp.square(xf - mu), -1, keepdims=True)
    y = (xf - mu) * lax.rsqrt(var + LN_EPS)
    return (y * g.astype(jnp.float32) + b.astype(jnp.float32)).astype(x.dtype)

def rope_tables(positions, dim):
    inv = ROPE_THETA ** (-jnp.arange(0, dim, 2, dtype=jnp.float32) / dim)
    ang = positions.astype(jnp.float32)[..., None] * inv
    ang = jnp.concatenate([ang, ang], -1)[:, :, None, :]
    return jnp.cos(ang), jnp.sin(ang)

def apply_rope(t, cos, sin):
    t1, t2 = jnp.split(t, 2, axis=-1)
    rot = jnp.concatenate([-t2, t1], -1)
    return (t.astype(jnp.float32) * cos + rot.astype(jnp.float32) * sin).astype(t.dtype)

def chunk_relpos_attention(q, k, v, rel_bias):
    Bn, S, H, Dh = q.shape
    nc = S // CHUNK
    qc = q.reshape(Bn, nc, CHUNK, H, Dh)

    def band(t):
        t = t.reshape(Bn, nc, CHUNK, H, Dh)
        tp = jnp.pad(t, ((0, 0), (LEFT_CHUNKS, 0), (0, 0), (0, 0), (0, 0)))
        return jnp.concatenate([tp[:, j:j + nc] for j in range(N_BAND)], axis=2)

    kb, vb = band(k), band(v)
    s = jnp.einsum('bnqhd,bnkhd->bnhqk', qc, kb).astype(jnp.float32) * (Dh ** -0.5)
    qi = jnp.arange(CHUNK)[:, None]
    slot = jnp.arange(N_BAND * CHUNK)[None, :]
    dist = LEFT_CHUNKS * CHUNK + qi - slot
    bias = rel_bias[:, jnp.clip(dist, -REL_CLIP, REL_CLIP) + REL_CLIP]
    key_chunk = jnp.arange(nc)[:, None] - LEFT_CHUNKS + slot // CHUNK
    s = s + bias.astype(jnp.float32)[None, None]
    s = jnp.where((key_chunk >= 0)[None, :, None, None, :], s, NEG)
    pr = jax.nn.softmax(s, axis=-1).astype(v.dtype)
    o = jnp.einsum('bnhqk,bnkhd->bnqhd', pr, vb)
    return o.reshape(Bn, S, H * Dh)

def indexed_sparse_attention(q, k, v, q_idx, k_idx, w_idx, topk):
    Bn, S = q.shape[:2]
    nb = S // Q_BLOCK
    key_pos = jnp.arange(S)

    def blockify(t):
        return jnp.moveaxis(t.reshape((Bn, nb, Q_BLOCK) + t.shape[2:]), 1, 0)

    def one_block(args):
        blk, qb, qib, wib = args
        t = blk * Q_BLOCK + jnp.arange(Q_BLOCK)
        visible_end = (t // CHUNK + 1) * CHUNK
        admissible = key_pos[None, :] < visible_end[:, None]
        dots = jnp.einsum('bqhd,bsd->bqhs', qib, k_idx).astype(jnp.float32) * (D_IDX ** -0.5)
        score = jnp.einsum('bqh,bqhs->bqs', wib.astype(jnp.float32) * (H_IDX ** -0.5), jax.nn.relu(dots))
        score = jnp.where(admissible[None], score, NEG)
        top_val, top_idx = lax.top_k(score, topk)
        sel_valid = top_val > 0.5 * NEG
        k_sel = jax.vmap(lambda kk, ii: kk[ii])(k, top_idx)
        v_sel = jax.vmap(lambda vv, ii: vv[ii])(v, top_idx)
        s = jnp.einsum('bqhd,bqkd->bhqk', qb, k_sel).astype(jnp.float32) * (HEAD_DIM ** -0.5)
        s = jnp.where(sel_valid[:, None], s, NEG)
        pr = jax.nn.softmax(s, axis=-1).astype(v.dtype)
        return jnp.einsum('bhqk,bqkd->bqhd', pr, v_sel)

    out = lax.map(one_block, (jnp.arange(nb), blockify(q), blockify(q_idx), blockify(w_idx)))
    return jnp.moveaxis(out, 0, 1).reshape(Bn, S, H_B * HEAD_DIM)

def hybrid_layer(x, p_i, rope_h, rope_i, w_in, b_in, rel_bias, w_out, w_ple, w_pg, b_pg, ln_g, ln_b, topk):
    Bn, S, _ = x.shape
    cos_h, sin_h = rope_h
    cos_i, sin_i = rope_i
    proj = x @ w_in + b_in
    qa, ka, va, ga, qb, kb, vb, gb, qi, ki, wi = jnp.split(proj, SPLIT_IDX, axis=-1)
    ya = chunk_relpos_attention(qa.reshape(Bn, S, H_A, HEAD_DIM), ka.reshape(Bn, S, H_A, HEAD_DIM),
                                va.reshape(Bn, S, H_A, HEAD_DIM), rel_bias)
    qb = apply_rope(qb.reshape(Bn, S, H_B, HEAD_DIM), cos_h, sin_h)
    kb = apply_rope(kb.reshape(Bn, S, 1, HEAD_DIM), cos_h, sin_h).reshape(Bn, S, HEAD_DIM)
    qi = apply_rope(qi.reshape(Bn, S, H_IDX, D_IDX), cos_i, sin_i)
    ki = apply_rope(ki.reshape(Bn, S, 1, D_IDX), cos_i, sin_i).reshape(Bn, S, D_IDX)
    yb = indexed_sparse_attention(qb, kb, vb, qi, ki, wi, topk)
    y = jnp.concatenate([ya * jax.nn.silu(ga), yb * jax.nn.silu(gb)], axis=-1) @ w_out
    ple = jax.nn.sigmoid(x @ w_pg + b_pg) * (p_i @ w_ple)
    return layer_norm(ALPHA * x + y + ple, ln_g, ln_b)

def setup_inputs(seed: int = 0) -> dict:
    key = jax.random.key(seed)
    ks = jax.random.split(key, 14)
    f32 = jnp.float32
    x = jax.random.normal(ks[0], (BATCH, SEQ, D_MODEL), f32)
    p = jax.random.normal(ks[1], (DEPTH, BATCH, SEQ, D_PLE), f32)
    start = jax.random.randint(ks[2], (BATCH, 1), 0, 4096, dtype=jnp.int32)
    positions = start + jnp.arange(SEQ, dtype=jnp.int32)[None, :]
    col_scale = jnp.concatenate([jnp.full((n,), BETA if i in V_PARTS else 1.0, f32)
                                 for i, n in enumerate(SPLIT_SIZES)])
    w_in = jax.random.normal(ks[3], (DEPTH, D_MODEL, D_IN), f32) * (D_MODEL ** -0.5) * col_scale
    b_in = 0.01 * jax.random.normal(ks[4], (DEPTH, D_IN), f32)
    rel_bias = 0.2 * jax.random.normal(ks[5], (DEPTH, H_A, 2 * REL_CLIP + 1), f32)
    w_out = jax.random.normal(ks[6], (DEPTH, D_MIX, D_MODEL), f32) * (D_MIX ** -0.5) * BETA
    w_ple = jax.random.normal(ks[7], (DEPTH, D_PLE, D_MODEL), f32) * (D_PLE ** -0.5) * BETA
    w_ple_gate = jax.random.normal(ks[8], (DEPTH, D_MODEL, D_MODEL), f32) * (D_MODEL ** -0.5)
    b_ple_gate = 0.01 * jax.random.normal(ks[9], (DEPTH, D_MODEL), f32)
    ln_g = 1.0 + 0.02 * jax.random.normal(ks[10], (DEPTH, D_MODEL), f32)
    ln_b = 0.01 * jax.random.normal(ks[11], (DEPTH, D_MODEL), f32)
    return {'x': x, 'p': p, 'positions': positions, 'w_in': w_in, 'b_in': b_in, 'rel_bias': rel_bias,
            'w_out': w_out, 'w_ple': w_ple, 'w_ple_gate': w_ple_gate, 'b_ple_gate': b_ple_gate,
            'ln_g': ln_g, 'ln_b': ln_b}

def reference(x, p, positions, w_in, b_in, rel_bias, w_out, w_ple, w_ple_gate, b_ple_gate, ln_g, ln_b):
    S = x.shape[1]
    topk = min(TOPK_MAX, S // 4)
    rope_h = rope_tables(positions, HEAD_DIM)
    rope_i = rope_tables(positions, D_IDX)
    for i in range(DEPTH):
        x = hybrid_layer(x, p[i], rope_h, rope_i, w_in[i], b_in[i], rel_bias[i], w_out[i], w_ple[i],
                         w_ple_gate[i], b_ple_gate[i], ln_g[i], ln_b[i], topk)
    return x


_drawn_inputs = setup_inputs


def setup_inputs(seed=0):
    import zlib

    import numpy as np

    out = dict(_drawn_inputs(seed))
    spreads = {}
    factors = {'b_in': 8.0,
     'rel_bias': 8.0,
     'w_out': 3.039,
     'b_ple_gate': 54.87,
     'ln_g': 8.197,
     'ln_b': 16.649}
    for name, (base, spread) in spreads.items():
        noise = np.random.default_rng([zlib.crc32(name.encode()), seed]).standard_normal(out[name].shape)
        drawn = base * np.exp(spread * noise) if base else spread * noise
        out[name] = __import__('jax').numpy.asarray(drawn.astype(out[name].dtype))
    for name, factor in factors.items():
        out[name] = (out[name] * factor).astype(out[name].dtype)
    return out
```

```python
from contextlib import ExitStack

import numpy as np

import concourse.bass as bass
from concourse import mybir

F32 = mybir.dt.float32
F32R = mybir.dt.float32r
BF16 = mybir.dt.bfloat16
I32 = mybir.dt.int32
ALU = mybir.AluOpType
ACT = mybir.ActivationFunctionType

P = 128
SEQ = 1024
D_MODEL = 2048
D_IN = 6984
D_PLE = 256
CHUNK = 64
HEAD_DIM = 128
H_A = 8
H_B = 8
H_IDX = 8
D_IDX = 64
TOPK = 256
REL_CLIP = 128
N_REL = 2 * REL_CLIP + 1
ROPE_THETA = 10000.0
LN_EPS = 1e-5
ALPHA = 2.0 ** 0.25
NEG = -1e30
TAKEN = -3e38

KT = D_MODEL // P
ST = SEQ // P
HALF = SEQ // 2
COL = 512
BIAS_COLS = D_IN // P
COL_QA, COL_KA, COL_VA, COL_GA, COL_QB, COL_KB, COL_VB, COL_GB, COL_QI = 0, 8, 16, 24, 32, 40, 41, 42, 50
COL_KW = BIAS_COLS * P
KW = D_IDX + H_IDX
FIRST_PICKED = TOPK // P
BAND_TILES = 5
MASK_AT = [P, 0] + [2 * P + sum((j + 1) * P for j in range(FIRST_PICKED, b)) for b in range(FIRST_PICKED, ST)]
MASK_COLS = MASK_AT[-1] + SEQ
SCORE_AT = [None, None] + [m - 2 * P for m in MASK_AT[2:]]
SCORE_COLS = MASK_COLS - 2 * P

TWO_PI_1 = 6.28125
TWO_PI_2 = float(np.float32(round((2 * np.pi - TWO_PI_1) * 2 ** 20) / 2 ** 20))
TWO_PI_3 = float(np.float32(2 * np.pi - TWO_PI_1 - TWO_PI_2))
ROUND = 1.5 * 2 ** 23
PI_BELOW = 3.1415925


def hold(eng, sem, value):
    eng.wait_ge(sem, value)
    eng.nop(nofuse=True)


class Store:

    def __init__(self, nc, ctx):
        self.nc, self.ctx = nc, ctx

    def sb(self, name, shape, dt=F32):
        return self.ctx.enter_context(self.nc.sbuf_tensor(name, shape, dt))

    def ps(self, name, shape):
        return self.ctx.enter_context(self.nc.psum_tensor(name, shape, F32))


class Chain:

    def __init__(self, eng, sem):
        self.eng, self.sem, self.n, self.base = eng, sem, 0, 0

    def step(self, ins):
        ins.then_inc(self.sem, 1)
        self.n += 1

    def wait(self):
        hold(self.eng, self.sem, self.base + self.n)

    def link(self, ins):
        self.step(ins)
        self.wait()

    def enter(self, i, per):
        self.start, self.per, self.base, self.n = self.base + self.n, per, self.base + self.n + i * per, 0

    def leave(self, count):
        assert self.n == self.per, self.n
        self.base, self.n = self.start + count * self.per, 0


def f(ap):
    return ap.bitcast(F32)


def matmul3(nc, out, l_hi, l_lo, r_hi, r_lo, start, stop, **kw):
    nc.tensor.matmul(out, l_hi, r_hi, start=start, stop=False, **kw)
    nc.tensor.matmul(out, l_hi, r_lo, start=False, stop=False, **kw)
    return nc.tensor.matmul(out, l_lo, r_hi, start=False, stop=stop, **kw)


def load_block(nc, sem, m, io):
    with ExitStack() as ctx:
        st = Store(nc, ctx)
        x_row = st.sb("x_row", [P, 2, D_MODEL])
        b_row = st.sb("b_row", [BIAS_COLS, P])
        pos_i = st.sb("pos_i", [P, SEQ], I32)
        pos = st.sb("pos", [P, SEQ])
        ang = st.sb("ang", [P, SEQ])
        turns = st.sb("turns", [P, SEQ])
        rest = st.sb("rest", [P, SEQ])
        freq = st.sb("freq", [P, 4])
        head_tab = st.sb("head_tab", [P, 2, SEQ])
        rel = st.sb("rel", [H_A, 3 * P])
        x_ps = st.ps("x_ps", [P, 4, 4, P])
        b_ps = st.ps("b_ps", [P, COL])

        ident_zero, ident_ok = sem("ident_zero"), sem("ident_ok")
        x_in = [sem("x_in0"), sem("x_in1")]
        small_in, b_turned, b_ok = sem("small_in"), sem("b_turned"), sem("b_ok")
        x_turned, x_hi_ok, x_free = sem("x_turned"), sem("x_hi_ok"), sem("x_free")
        tab_steps, rest_ok, tab_ok, head_tab_out = sem("tab_steps"), sem("rest_ok"), sem("tab_ok"), sem("head_tab_out")
        rel_in, rel_ok, rel_out = sem("rel_in"), sem("rel_ok"), sem("rel_out")
        x_rows = io["x"].rearrange("(t p) d -> t p d", p=P)
        tables = [(0, m.sin_i, 0.0), (0, m.cos_i, 0.25), (1, head_tab[:, 0, :], 0.0), (1, head_tab[:, 1, :], 0.25)]

        with nc.Block() as block:
            @block.sync
            def _(sp):
                for j in range(2):
                    sp.dma_start(x_row[:, j, :], x_rows[j]).then_inc(x_in[j], 16)
                with sp.Fori(1, ST // 2) as i:
                    for j in range(2):
                        sp.wait_ge(x_free, 4 * (i * 2 + j))
                        sp.dma_start(x_row[:, j, :], x_rows[bass.ds(i * 2 + j, 1), :, :].rearrange("t p d -> p (t d)")) \
                            .then_inc(x_in[j], 16)

                sp.wait_ge(rel_ok, 1)
                sp.dma_start(io["rel_pad"][:, 0:3 * P - 1], rel[:, 0:3 * P - 1]).then_inc(rel_out, 16)
                sp.wait_ge(rel_out, 16)
                pad = io["rel_pad"]
                sp.dma_start(io["rel_skew"], bass.AP(tensor=pad.tensor, offset=pad.offset + P - 1,
                                                     ap=[[3 * P, H_A], [-1, P], [1, 2 * P]])).then_inc(rel_out, 16)
                sp.wait_ge(rel_out, 32)

            @block.gpsimd
            def _(pool):
                nc.gpsimd.memset(m.ident, 0.0).then_inc(ident_zero, 1)
                pool.wait_ge(ident_zero, 1)
                nc.gpsimd.affine_select(out=m.ident, in_=m.ident, compare_op=ALU.not_equal, fill=1.0, base=0,
                                        pattern=[[-1, P]], channel_multiplier=1).then_inc(ident_ok, 1)

            @block.tensor
            def _(pe):
                pe.wait_ge(ident_ok, 1)
                with pe.Fori(0, ST // 2) as i:
                    for j in range(2):
                        pe.wait_ge(x_in[j], 16 * (i + 1))
                        for g in range(4):
                            pe.wait_ge(x_free, 4 * (i * 2 + j) + g + 1)
                            for k in range(4):
                                last = nc.tensor.transpose(x_ps[:, g, k, :], x_row[:, j, bass.ts(4 * g + k, P)], m.ident)
                            last.then_inc(x_turned, 1)
                pe.wait_ge(small_in, 64)
                nc.tensor.transpose(b_ps[:, 0:BIAS_COLS], b_row[:], m.ident[0:BIAS_COLS, 0:BIAS_COLS]).then_inc(b_turned, 1)

            @block.scalar
            def _(act):
                act.dma_start(pos_i[:], io["positions"].partition_broadcast(P)).then_inc(small_in, 16)
                act.dma_start(freq[:], io["rotary"]).then_inc(small_in, 16)
                act.dma_start(b_row[:], io["b_in"][0:BIAS_COLS * P].rearrange("(t p) -> t p", p=P)).then_inc(small_in, 16)
                act.dma_start(rel[:, P - 1:3 * P - 1], io["rel_bias"][:, N_REL - 1:0:-1], allow_slow_non_contiguous=True) \
                    .then_inc(rel_in, 16)
                act.dma_start(m.kw_bias, io["b_in"][COL_KW:D_IN].rearrange("(p a) -> p a", a=1)).then_inc(small_in, 16)
                with act.Fori(0, ST // 2) as i:
                    for j in range(2):
                        s = i * 2 + j
                        for g in range(4):
                            act.wait_ge(x_turned, 4 * s + g + 1)
                            nc.scalar.copy(m.x_hi[:, 4 * g:4 * g + 4, bass.ds(s * P, P)], x_ps[:, g, :, :]).then_inc(x_hi_ok, 1)
                for n, (_, out, _) in enumerate(tables):
                    act.wait_ge(rest_ok, n + 1)
                    nc.scalar.activation(out, rest[:], ACT.Sin).then_inc(tab_ok, 1)
                act.wait_ge(tab_ok, 4)
                act.dma_start(io["head_tab"].rearrange("c p s -> p c s"), head_tab[:]).then_inc(head_tab_out, 16)
                act.wait_ge(head_tab_out, 16)

            @block.vector
            def _(dve):
                dve.sem_inc(x_free, 4)
                with dve.Fori(0, ST // 2) as i:
                    for j in range(2):
                        s = i * 2 + j
                        for g in range(4):
                            dve.wait_ge(x_hi_ok, 4 * s + g + 1)
                            part = (slice(None), slice(4 * g, 4 * g + 4), bass.ds(s * P, P))
                            nc.vector.tensor_tensor(m.x_lo[part], x_ps[:, g, :, :], f(m.x_hi[part]), ALU.subtract) \
                                .then_inc(x_free, 1)
                dve.wait_ge(rel_in, 16)
                nc.vector.tensor_copy(rel[:, 0:P - 1], rel[:, P - 1:P].to_broadcast([H_A, P - 1])).then_inc(rel_ok, 1)
                ch = Chain(dve, tab_steps)
                dve.wait_ge(small_in, 64)
                ch.link(nc.vector.tensor_copy(pos[:], pos_i[:]))
                for n, (width, _, quarter) in enumerate(tables):
                    if quarter == 0.0:
                        ch.link(nc.vector.tensor_scalar(ang[:], pos[:], freq[:, width:width + 1], None, ALU.mult))
                    ch.link(nc.vector.tensor_scalar(turns[:], ang[:], 1.0 / (2 * np.pi), quarter, ALU.mult, ALU.add))
                    ch.link(nc.vector.tensor_scalar(turns[:], turns[:], ROUND, -ROUND, ALU.add, ALU.add))
                    if n:
                        dve.wait_ge(tab_ok, n)
                    ch.link(nc.vector.scalar_tensor_tensor(rest[:], turns[:], -TWO_PI_1, ang[:], ALU.mult, ALU.add))
                    ch.link(nc.vector.scalar_tensor_tensor(rest[:], turns[:], -TWO_PI_2, rest[:], ALU.mult, ALU.add))
                    ch.link(nc.vector.scalar_tensor_tensor(rest[:], turns[:], -TWO_PI_3, rest[:], ALU.mult, ALU.add))
                    if quarter:
                        ch.link(nc.vector.tensor_scalar(rest[:], rest[:], 0.5 * np.pi, None, ALU.add))
                    else:
                        ch.link(nc.vector.tensor_scalar(rest[:], rest[:], freq[:, 2 + width:3 + width], None, ALU.mult))
                    nc.vector.tensor_scalar(rest[:], rest[:], PI_BELOW, -PI_BELOW, ALU.min, ALU.max).then_inc(rest_ok, 1)
                dve.wait_ge(b_turned, 1)
                nc.vector.tensor_copy(m.b_col, b_ps[:, 0:BIAS_COLS]).then_inc(b_ok, 1)
                dve.wait_ge(b_ok, 1)
                nc.vector.tensor_scalar(m.b_neg, m.b_col, -1.0, None, ALU.mult).then_inc(b_ok, 1)
                dve.wait_ge(b_ok, 2)


def index_block(nc, sem, m, io):
    with ExitStack() as ctx:
        st = Store(nc, ctx)
        RAW, PART = 2, 4
        w_raw = st.sb("iw_raw", [P, RAW, 4, P])
        w_hi = st.sb("iw_hi", [P, PART, 4, P], F32R)
        w_lo = st.sb("iw_lo", [P, PART, 4, P], F32R)
        ki_hi = st.sb("ki_hi", [P, SEQ], F32R)
        ki_lo = st.sb("ki_lo", [P, SEQ], F32R)
        qi_hi = st.sb("qi_hi", [P, 2, SEQ], F32R)
        qi_lo = st.sb("qi_lo", [P, 2, SEQ], F32R)
        plain = st.sb("i_plain", [P, COL])
        swapped = st.sb("i_swapped", [P, COL])
        w_idx = st.sb("w_idx", [P, ST, H_IDX])
        proj = st.ps("i_proj", [P, 2, COL])
        dots = [st.ps(f"i_dots{n}", [P, 2, COL]) for n in range(3)]
        w_ps = dots[2]

        raw_in = [sem("iw_in0"), sem("iw_in1")]
        hi_ok, lo_ok, chunk_used = sem("iw_hi_ok"), sem("iw_lo_ok"), sem("iw_used")
        plain_ok, proj_free = sem("i_plain_ok"), sem("i_proj_free")
        rope_steps, roped, part_hi_ok, part_lo_ok = sem("i_rope_steps"), sem("i_roped"), sem("i_part_hi"), sem("i_part_lo")
        ki_both, wi_turned, wi_ok = sem("ki_both"), sem("wi_turned"), sem("wi_ok")
        dots_ok, relu_ok, score_ok, corner_ok = sem("dots_ok"), sem("relu_ok"), sem("score_ok"), sem("corner_ok")

        TILES = 5
        cols = [(COL_KW, KW)] + [((COL_QI + t) * P, P) for t in range(4)]
        w_rows = io["w_in"].rearrange("(c k p) n -> c p k n", k=4, p=P)
        steps = [(t, hh, b) for t in range(4) for b in range(FIRST_PICKED, ST) for hh in range(2)]
        PER_TILE = len(steps) // 4

        with nc.Block() as block:
            @block.sync
            def _(sp):
                for t, (c0, n) in enumerate(cols):
                    for c in range(4):
                        k = 4 * t + c
                        if k >= RAW:
                            sp.wait_ge(lo_ok, k - RAW + 1)
                        sp.dma_start(w_raw[:, k % RAW, :, 0:n], w_rows[c, :, :, c0:c0 + n]).then_inc(raw_in[k % RAW], 16)
                    if t == 1:
                        sp.wait_ge(part_lo_ok, 2)
                        sp.dma_start(f(ki_hi[D_IDX:P, :]), f(ki_hi[0:D_IDX, :])).then_inc(ki_both, 16)
                        sp.dma_start(f(ki_lo[D_IDX:P, :]), f(ki_lo[0:D_IDX, :])).then_inc(ki_both, 16)

            def parts(t, h):
                at = slice(h * COL, (h + 1) * COL)
                if t == 0:
                    return ki_hi[0:D_IDX, at], ki_lo[0:D_IDX, at]
                return qi_hi[:, (t - 1) % 2, at], qi_lo[:, (t - 1) % 2, at]

            def split_hi(act, k):
                n = cols[k // 4][1]
                act.wait_ge(raw_in[k % RAW], 16 * (k // RAW + 1))
                if k >= PART:
                    act.wait_ge(chunk_used, k - PART + 1)
                nc.scalar.copy(w_hi[:, k % PART, :, 0:n], w_raw[:, k % RAW, :, 0:n]).then_inc(hi_ok, 1)

            @block.gpsimd
            def _(pool):
                for k in range(4 * TILES):
                    n = cols[k // 4][1]
                    pool.wait_ge(hi_ok, k + 1)
                    nc.gpsimd.tensor_tensor(w_lo[:, k % PART, :, 0:n], w_raw[:, k % RAW, :, 0:n],
                                            f(w_hi[:, k % PART, :, 0:n]), ALU.subtract).then_inc(lo_ok, 1)

            @block.scalar
            def _(act):
                for k in range(2):
                    split_hi(act, k)

                def tile(t):
                    n = cols[t][1]
                    for c in range(4):
                        if 4 * t + c + 2 < 4 * TILES:
                            split_hi(act, 4 * t + c + 2)
                    bias = m.kw_bias if t == 0 else m.b_col[:, COL_QI + t - 1:COL_QI + t]
                    for h in range(2):
                        act.wait_ge(chunk_used, 4 * (t + 1))
                        if 2 * t + h >= 1:
                            act.wait_ge(part_lo_ok, 2 * t + h)
                        if t == 0 and h == 1:
                            act.wait_ge(wi_turned, 1)
                        nc.scalar.activation(plain[0:n, :], proj[0:n, h, :], ACT.Identity, bias=bias[0:n, :])
                        for q in range(n // 32):
                            o = q ^ 1
                            last = nc.scalar.activation(swapped[32 * q:32 * q + 32, :], proj[32 * o:32 * o + 32, h, :],
                                                        ACT.Identity, bias=bias[32 * o:32 * o + 32, :])
                        last.then_inc(plain_ok, 1)
                        act.wait_ge(roped, 2 * t + h + 1)
                        hi, _ = parts(t, h)
                        nc.scalar.copy(hi, plain[0:hi.shape[0], :]).then_inc(part_hi_ok, 1)

                def relu(n):
                    t, hh, b = steps[n]
                    act.wait_ge(dots_ok, n + 1)
                    w = (b + 1) * P
                    d = dots[n % 3][:].rearrange("p a c -> p (a c)")[:, 0:w]
                    nc.scalar.activation(d, d, ACT.Relu, scale=D_IDX ** -0.5).then_inc(relu_ok, 1)

                tile(0)
                tile(1)
                for t in range(2, TILES):
                    tile(t)
                    for n in range((t - 2) * PER_TILE, (t - 1) * PER_TILE):
                        relu(n)
                for n in range(3 * PER_TILE, 4 * PER_TILE):
                    relu(n)

            @block.vector
            def _(dve):
                ch = Chain(dve, rope_steps)

                def tile(t):
                    r = D_IDX if t == 0 else P
                    if t >= 3:
                        dve.wait_ge(dots_ok, (t - 2) * PER_TILE)
                    for h in range(2):
                        at = slice(h * COL, (h + 1) * COL)
                        dve.wait_ge(plain_ok, 2 * t + h + 1)
                        if t == 0:
                            dve.wait_ge(wi_turned, h + 1)
                            nc.vector.tensor_scalar(w_idx[:, 4 * h:4 * h + 4, :],
                                                    w_ps[:, h, 0:4 * H_IDX].rearrange("p (j n) -> p j n", n=H_IDX),
                                                    H_IDX ** -0.5, None, ALU.mult).then_inc(wi_ok, 1)
                        ch.step(nc.vector.tensor_tensor(plain[0:r, :], plain[0:r, :], m.cos_i[0:r, at], ALU.mult))
                        ch.link(nc.vector.tensor_tensor(swapped[0:r, :], swapped[0:r, :], m.sin_i[0:r, at], ALU.mult))
                        nc.vector.tensor_tensor(plain[0:r, :], plain[0:r, :], swapped[0:r, :], ALU.add).then_inc(roped, 1)
                        hi, lo = parts(t, h)
                        dve.wait_ge(part_hi_ok, 2 * t + h + 1)
                        nc.vector.tensor_tensor(lo, plain[0:r, :], f(hi), ALU.subtract).then_inc(part_lo_ok, 1)

                def score(n):
                    t, hh, b = steps[n]
                    head, w = 2 * t + hh, (b + 1) * P
                    at = m.scores[:, SCORE_AT[b]:SCORE_AT[b] + w]
                    d = dots[n % 3][:].rearrange("p a c -> p (a c)")[:, 0:w]
                    wi = w_idx[:, b, head:head + 1]
                    dve.wait_ge(relu_ok, n + 1)
                    if head == 0:
                        nc.vector.tensor_scalar(at, d, wi, None, ALU.mult).then_inc(score_ok, 1)
                        return
                    dve.wait_ge(score_ok, n if hh else n - PER_TILE + 2)
                    nc.vector.scalar_tensor_tensor(at, d, wi, at, ALU.mult, ALU.add).then_inc(score_ok, 1)

                tile(0)
                dve.wait_ge(wi_ok, 2)
                tile(1)
                for t in range(2, TILES):
                    tile(t)
                    for n in range((t - 2) * PER_TILE, (t - 1) * PER_TILE):
                        score(n)
                for n in range(3 * PER_TILE, 4 * PER_TILE):
                    score(n)
                dve.wait_ge(score_ok, 4 * PER_TILE)
                for b in range(FIRST_PICKED, ST):
                    end = SCORE_AT[b] + (b + 1) * P
                    nc.vector.memset(m.scores[0:CHUNK, end - CHUNK:end], NEG).then_inc(corner_ok, 1)
                dve.wait_ge(corner_ok, ST - FIRST_PICKED)

            @block.tensor
            def _(pe):
                def project(t):
                    n = cols[t][1]
                    if t:
                        pe.wait_ge(part_lo_ok, 2 * t)
                    for c in range(4):
                        k = 4 * t + c
                        pe.wait_ge(lo_ok, k + 1)
                        for kk in range(4):
                            for h in range(2):
                                at = slice(h * COL, (h + 1) * COL)
                                kt = 4 * c + kk
                                last = matmul3(nc, proj[0:n, h, :], w_hi[:, k % PART, kk, 0:n], w_lo[:, k % PART, kk, 0:n],
                                               m.x_hi[:, kt, at], m.x_lo[:, kt, at], kt == 0, kt == KT - 1)
                        last.then_inc(chunk_used, 1)

                def dot(n):
                    t, hh, b = steps[n]
                    if n >= 3:
                        pe.wait_ge(score_ok, n - 2)
                    if n % PER_TILE == 0:
                        pe.wait_ge(part_lo_ok, 2 * (t + 2))
                    rows, at = slice(D_IDX * hh, D_IDX * hh + D_IDX), slice(b * P, b * P + P)
                    for c0 in range(0, (b + 1) * P, COL):
                        c1 = min(c0 + COL, (b + 1) * P)
                        last = matmul3(nc, dots[n % 3][:, c0 // COL, 0:c1 - c0], qi_hi[rows, t % 2, at], qi_lo[rows, t % 2, at],
                                       ki_hi[rows, c0:c1], ki_lo[rows, c0:c1], True, True)
                    last.then_inc(dots_ok, 1)

                project(0)
                for h in range(2):
                    pe.wait_ge(plain_ok, h + 1)
                    for j in range(4):
                        last = nc.tensor.transpose(w_ps[:, h, bass.ts(j, H_IDX)], plain[D_IDX:KW, bass.ts(j, P)],
                                                   m.ident[D_IDX:KW, D_IDX:KW])
                    last.then_inc(wi_turned, 1)
                project(1)
                pe.wait_ge(ki_both, 32)
                pe.wait_ge(wi_ok, 2)
                for t in range(2, TILES):
                    project(t)
                    for n in range((t - 2) * PER_TILE, (t - 1) * PER_TILE):
                        dot(n)
                for n in range(3 * PER_TILE, 4 * PER_TILE):
                    dot(n)


def gate_block(nc, sem, m, io):
    with ExitStack() as ctx:
        st = Store(nc, ctx)
        SLOTS = 3
        w_raw = st.sb("gw_raw", [P, SLOTS, COL])
        w_hi = st.sb("gw_hi", [P, SLOTS, COL], F32R)
        w_lo = st.sb("gw_lo", [P, SLOTS, COL], F32R)
        pt_hi = st.sb("pt_hi", [P, D_PLE // P, SEQ], F32R)
        pt_lo = st.sb("pt_lo", [P, D_PLE // P, SEQ], F32R)
        term = st.sb("term", [P, ST, COL])
        p_row = term[:, 0:4, :].rearrange("p a (b c) -> p (a b) c", b=2)
        bias = st.sb("pg_bias", [P, COL])
        best = st.sb("best", [P, ST, 8])
        bank = [st.ps(f"g_bank{s}", [P, COL]) for s in range(ST)]

        NP, NG = D_PLE // P, KT
        CH = NP + NG
        BLOCKS = D_MODEL // COL
        ROUNDS = TOPK // 8 // BLOCKS
        PICKED = ST - FIRST_PICKED
        p_in, bias_in = sem("p_in"), sem("pg_bias_in")
        raw_in = [sem(f"gw_in{n}") for n in range(SLOTS)]
        hi_ok, lo_ok, chunk_used = sem("gw_hi_ok"), sem("gw_lo_ok"), sem("gw_used")
        p_turned, p_hi_ok, p_lo_ok = sem("p_turned"), sem("p_hi_ok"), sem("p_lo_ok")
        ple_done, ple_ok, gate_done, biased, sigmoid_ok, bank_free = (
            sem("ple_done"), sem("ple_ok"), sem("gate_done"), sem("g_biased"), sem("sigmoid_ok"), sem("g_bank_free"))
        term_out, pick_steps = sem("term_out"), sem("pick_steps")
        out_cols = io["gate_term"].rearrange("(t p) n -> p t n", p=P)

        with nc.Block() as block:
            @block.sync
            def _(sp):
                sp.dma_start(p_row, io["p"].rearrange("(t p) d -> p t d", p=P)).then_inc(p_in, 16)

                with sp.Fori(0, BLOCKS) as i:
                    for c in range(CH):
                        sp.wait_ge(lo_ok, i * CH + c + 1)
                        rows = io["w_ple"][c * P:(c + 1) * P] if c < NP else io["w_pg"][(c - NP) * P:(c - NP + 1) * P]
                        sp.dma_start(w_raw[:, c % SLOTS, :], rows[:, bass.ds(i * COL, COL)]).then_inc(raw_in[c % SLOTS], 16)
                        if c == SLOTS:
                            sp.wait_ge(bank_free, (i + 1) * ST)
                            sp.dma_start(bias[:], io["b_pg"][bass.ds(i * COL, COL)].partition_broadcast(P)).then_inc(bias_in, 16)

            @block.gpsimd
            def _(pool):
                pool.sem_inc(lo_ok, SLOTS)
                with pool.Fori(0, BLOCKS) as i:
                    for c in range(CH):
                        pool.wait_ge(hi_ok, i * CH + c + 1)
                        nc.gpsimd.tensor_tensor(w_lo[:, c % SLOTS, :], w_raw[:, c % SLOTS, :], f(w_hi[:, c % SLOTS, :]),
                                                ALU.subtract).then_inc(lo_ok, 1)

            @block.tensor
            def _(pe):
                pe.wait_ge(p_in, 16)
                for s in range(ST):
                    for k in range(NP):
                        last = nc.tensor.transpose(bank[s][:, bass.ts(k, P)], p_row[:, s, bass.ts(k, P)], m.ident)
                    last.then_inc(p_turned, 1)
                pe.wait_ge(p_lo_ok, ST)
                with pe.Fori(0, BLOCKS) as i:
                    for c in range(CH):
                        pe.wait_ge(lo_ok, i * CH + c + 1 + SLOTS)
                        for s in range(ST):
                            at = bass.ts(s, P)
                            if c == 0:
                                pe.wait_ge(bank_free, i * ST + s + 1)
                            if c == NP:
                                pe.wait_ge(ple_ok, i * ST + s + 1)
                            if c < NP:
                                last = matmul3(nc, bank[s][:], pt_hi[:, c, at], pt_lo[:, c, at], w_hi[:, c % SLOTS, :],
                                               w_lo[:, c % SLOTS, :], c == 0, c == NP - 1)
                            else:
                                k = c - NP
                                last = matmul3(nc, bank[s][:], m.x_hi[:, k, at], m.x_lo[:, k, at], w_hi[:, c % SLOTS, :],
                                               w_lo[:, c % SLOTS, :], k == 0, k == NG - 1)
                            if c == NP - 1:
                                last.then_inc(ple_done, 1)
                            elif c == CH - 1:
                                last.then_inc(gate_done, 1)
                            elif s == ST - 1:
                                last.then_inc(chunk_used, 1)

            counted = [c for c in range(CH) if c not in (NP - 1, CH - 1)]

            @block.scalar
            def _(act):
                def split_hi(i, c):
                    c, i = c % CH, i + c // CH
                    act.wait_ge(raw_in[c % SLOTS], 16 * (i * (CH // SLOTS) + c // SLOTS + 1))
                    old = c - SLOTS
                    if old % CH == NP - 1:
                        act.wait_ge(ple_done, (i + old // CH + 1) * ST)
                    elif old % CH == CH - 1:
                        if not (isinstance(i, int) and i == 0):
                            act.wait_ge(gate_done, i * ST)
                    elif old >= 0 or not (isinstance(i, int) and i == 0):
                        before = (i + old // CH) * len(counted) + counted.index(old % CH) + 1
                        act.wait_ge(chunk_used, before)
                    nc.scalar.copy(w_hi[:, c % SLOTS, :], w_raw[:, c % SLOTS, :]).then_inc(hi_ok, 1)

                def column_block(i, last):
                    for c in range(CH):
                        if c + 2 < CH or not last:
                            split_hi(i, c + 2)
                        if c == NP - 1:
                            if not (isinstance(i, int) and i == 0):
                                act.wait_ge(term_out, 16 * i)
                            for s in range(ST):
                                act.wait_ge(ple_done, i * ST + s + 1)
                                nc.scalar.copy(term[:, s, :], bank[s][:]).then_inc(ple_ok, 1)
                    for s in range(ST):
                        act.wait_ge(biased, i * ST + s + 1)
                        nc.scalar.activation(bank[s][:], bank[s][:], ACT.Sigmoid).then_inc(sigmoid_ok, 1)
                    act.wait_ge(bank_free, (i + 2) * ST)
                    act.dma_start(out_cols[:, :, bass.ds(i * COL, COL)], term[:]).then_inc(term_out, 16)

                for s in range(ST):
                    act.wait_ge(p_turned, s + 1)
                    nc.scalar.copy(pt_hi[:, :, bass.ts(s, P)], bank[s][:, 0:NP * P].rearrange("p (k q) -> p k q", k=NP)) \
                        .then_inc(p_hi_ok, 1)
                split_hi(0, 0)
                split_hi(0, 1)
                column_block(0, False)
                with act.Fori(1, BLOCKS - 1) as i:
                    column_block(i, False)
                column_block(BLOCKS - 1, True)
                act.wait_ge(term_out, 16 * BLOCKS)

            @block.vector
            def _(dve):
                dve.sem_inc(bank_free, ST)
                for s in range(ST):
                    dve.wait_ge(p_hi_ok, s + 1)
                    part = (slice(None), slice(None), bass.ts(s, P))
                    nc.vector.tensor_tensor(pt_lo[part], bank[s][:, 0:NP * P].rearrange("p (k q) -> p k q", k=NP),
                                            f(pt_hi[part]), ALU.subtract).then_inc(p_lo_ok, 1)
                ch = Chain(dve, pick_steps)

                def rounds(first, n):
                    group = [FIRST_PICKED + (first + j) % PICKED for j in range(n)]
                    for b in group:
                        at = m.scores[:, SCORE_AT[b]:SCORE_AT[b] + (b + 1) * P]
                        ch.step(nc.vector.max(best[:, b, :], at))
                    ch.wait()
                    for b in group:
                        at = m.scores[:, SCORE_AT[b]:SCORE_AT[b] + (b + 1) * P]
                        ch.step(nc.vector.match_replace(out=at, in_to_replace=best[:, b, :], in_values=at, imm_value=TAKEN))
                    ch.wait()

                EACH = PICKED * ROUNDS // KT
                with dve.Fori(0, BLOCKS) as i:
                    ch.enter(i, 2 * PICKED * ROUNDS)
                    for c in range(KT):
                        rounds(c * EACH, EACH)
                    dve.wait_ge(bias_in, 16 * (i + 1))
                    for s in range(ST + 1):
                        if s < ST:
                            dve.wait_ge(gate_done, i * ST + s + 1)
                            nc.vector.tensor_tensor(bank[s][:], bank[s][:], bias[:], ALU.add).then_inc(biased, 1)
                        if s:
                            dve.wait_ge(sigmoid_ok, i * ST + s)
                            nc.vector.tensor_tensor(term[:, s - 1, :], bank[s - 1][:], term[:, s - 1, :], ALU.mult) \
                                .then_inc(bank_free, 1)
                ch.leave(BLOCKS)
                for b in range(FIRST_PICKED, ST):
                    w = (b + 1) * P
                    ch.step(nc.vector.tensor_scalar(m.mask[:, MASK_AT[b]:MASK_AT[b] + w], m.scores[:, SCORE_AT[b]:SCORE_AT[b] + w],
                                                    0.5 * TAKEN, NEG, ALU.is_gt, ALU.mult))
                ch.link(nc.vector.memset(m.mask[:, 0:2 * P], 0.0))
                ch.link(nc.vector.memset(m.mask[0:CHUNK, 2 * P - CHUNK:2 * P], NEG))


class Turn:

    def __init__(self, tiles, head, group, chunk0, raw0, round0, parts0, reads0):
        self.tiles = tiles
        self.head = head
        self.group = group
        self.chunk0 = chunk0
        self.raw0 = raw0
        self.round0 = round0
        self.parts0 = parts0
        self.reads0 = reads0


QK_AT = [2, 4, 6, 9, 13, 17, 21, 25]
EXP_AT = [3, 5, 7, 10, 14, 18, 22, 26]
NORM_AT = [3, 5, 7, 10, 15, 19, 23, 27]
TURN_AT = [4, 6, 9, 13, 17, 21, 25, 29]
PV_AT = [6, 8, 11, 15, 20, 24, 28, 31]
ATTEND = 32


def block_rounds(b):
    return 1 + (b >= 4), b + max(0, b - 4)


HEAD_ROUNDS = sum(block_rounds(b)[0] for b in range(ST))
V_ROUNDS = 2


def heads_block(nc, sem, m, io):
    with ExitStack() as ctx:
        st = Store(nc, ctx)
        SLOTS, LEAD, KC = 4, 3, 2
        PER = KT // KC
        w_raw = st.sb("hw_raw", [P, SLOTS, KC, P])
        w_hi = st.sb("hw_hi", [P, SLOTS, KC, P], F32R)
        w_lo = st.sb("hw_lo", [P, SLOTS, KC, P], F32R)
        q_hi, q_lo = st.sb("q_hi", [P, SEQ], F32R), st.sb("q_lo", [P, SEQ], F32R)
        k_hi, k_lo = st.sb("k_hi", [P, SEQ], F32R), st.sb("k_lo", [P, SEQ], F32R)
        v_hi, v_lo = st.sb("v_hi", [P, SEQ], F32R), st.sb("v_lo", [P, SEQ], F32R)
        pt_hi, pt_lo = st.sb("h_pt_hi", [P, SEQ], F32R), st.sb("h_pt_lo", [P, SEQ], F32R)
        gate = st.sb("gate", [P, SEQ])
        prob = st.sb("prob", [P, SEQ])
        tab = st.sb("h_tab", [P, 2, SEQ])
        tmp = st.sb("h_tmp", [P, 2 * COL])
        band, toeplitz = tmp[:, 0:BAND_TILES * P], tmp[:, BAND_TILES * P:(BAND_TILES + 2) * P]
        plain, swapped = tmp[:, 0:COL], tmp[:, COL:2 * COL]
        low = st.sb("low", [P, ST])
        total = st.sb("total", [P, ST])
        inv = st.sb("inv", [P, ST])
        proj = [st.ps("h_proj0", [P, SEQ]), st.ps("h_proj1", [P, SEQ])]
        s_ps = st.ps("s_ps", [P, SEQ])
        t_ps = st.ps("t_ps", [P, COL])
        o_ps = st.ps("o_ps", [P, COL])

        raw_in = [sem(f"hw_in{n}") for n in range(SLOTS)]
        hi_ok, lo_ok, chunk_used = sem("hw_hi_ok"), sem("hw_lo_ok"), sem("hw_used")
        part_hi, part_lo, rope_read, roped, rope_steps = sem("h_part_hi"), sem("h_part_lo"), sem("h_rope_read"), sem("h_roped"), sem("h_rope_steps")
        v_read, gate_exp, gate_ok, gate_steps = sem("v_read"), sem("gate_exp"), sem("gate_ok"), sem("gate_steps")
        s_ok, low_ok, exp_ok, inv_ok, norm_ok = sem("s_ok"), sem("low_ok"), sem("exp_ok"), sem("inv_ok"), sem("norm_ok")
        turned, turned_hi, turned_lo, pv_ok, y_ok = sem("turned"), sem("turned_hi"), sem("turned_lo"), sem("pv_ok"), sem("y_ok")
        y_out, toep_in, band_steps, band_ok, tab_in = sem("y_out"), sem("toep_in"), sem("band_steps"), sem("band_ok"), sem("h_tab_in")
        SCALE = HEAD_DIM ** -0.5

        A_TURN, B_TURN = 4 * PER, 2 * PER

        def turn_a(h, peeled=False):
            tiles = [("q", COL_QA + h, False), ("k", COL_KA + h, False), ("v", COL_VA + h, False), ("g", COL_GA + h, False)]
            if peeled:
                return Turn(tiles, None, "A", 0, 0, 0, 0, 0)
            return Turn(tiles, h - 1, "A", h * A_TURN, h * (A_TURN // SLOTS),
                        (h - 1) * (HEAD_ROUNDS + V_ROUNDS) + V_ROUNDS, h * 4, 0)

        def turn_mid():
            tiles = [("q", COL_QB, True), ("k", COL_KB, True), ("v", COL_VB, False), ("g", COL_GB, False)]
            return Turn(tiles, H_A - 1, "A", H_A * A_TURN, H_A * A_TURN // SLOTS,
                        (H_A - 1) * (HEAD_ROUNDS + V_ROUNDS) + V_ROUNDS, H_A * 4, 0)

        def turn_b(j, last=False):
            tiles = [] if last else [("q", COL_QB + 1 + j, True), ("g", COL_GB + 1 + j, False)]
            c0 = (H_A + 1) * A_TURN
            return Turn(tiles, H_A + j, "B", j * B_TURN + c0, j * (B_TURN // SLOTS) + c0 // SLOTS,
                        j * HEAD_ROUNDS + (H_A * (HEAD_ROUNDS + V_ROUNDS) + V_ROUNDS), j * 2 + (H_A + 1) * 4, j * 2 + 4)

        def all_turns(eng, run):
            run(turn_a(0, peeled=True), True)
            with eng.Fori(1, H_A) as h:
                run(turn_a(h), True)
            run(turn_mid(), True)
            with eng.Fori(0, H_B - 2) as j:
                run(turn_b(j), True)
            run(turn_b(H_B - 2), False)
            run(turn_b(H_B - 1, last=True), False)

        def wait(eng, s, value):
            if not (isinstance(value, int) and value <= 0):
                eng.wait_ge(s, value)

        def blocks_before(t, b):
            return t.head * ST + b

        def width(t, b):
            n = min(b + 1, BAND_TILES) if t.group == "A" else b + 1
            return n, b + 1 - n

        def positions(t):
            return range(max(KT * len(t.tiles), ATTEND if t.head is not None else 0))

        def role_at(t, role):
            return KT * (1 + [r for r, _, _ in t.tiles].index(role))

        def has(t, role):
            return any(r == role for r, _, _ in t.tiles)

        def ropes(t, role):
            return any(r == role and rot for r, _, rot in t.tiles)

        w_rows = io["w_in"].rearrange("(c k p) n -> c p k n", k=KC, p=P)

        with nc.Block() as block:
            @block.sync
            def _(sp):
                sp.dma_start(tab[:], io["head_tab"].rearrange("c p s -> p c s")).then_inc(tab_in, 16)

                def run(t, more):
                    for c in range(PER * len(t.tiles)):
                        role, tile, _ = t.tiles[c // PER]
                        wait(sp, lo_ok, t.chunk0 + (c - SLOTS + 1))
                        sp.dma_start(w_raw[:, c % SLOTS, :, :], w_rows[c % PER, :, :, bass.ds(tile * P, P)]) \
                            .then_inc(raw_in[c % SLOTS], 16)
                        if c == 4 and t.group == "A" and not ropes(t, "q"):
                            h = 0 if t.head is None else t.head + 1
                            wait(sp, band_ok, h)
                            sp.dma_start(toeplitz, io["rel_skew"][bass.ds(h, 1), :, :].rearrange("h p n -> p (h n)")) \
                                .then_inc(toep_in, 16)
                all_turns(sp, run)

            @block.gpsimd
            def _(pool):
                def run(t, more):
                    for c in range(PER * len(t.tiles)):
                        pool.wait_ge(hi_ok, t.chunk0 + (c + 1))
                        nc.gpsimd.tensor_tensor(w_lo[:, c % SLOTS, :, :], w_raw[:, c % SLOTS, :, :],
                                                f(w_hi[:, c % SLOTS, :, :]), ALU.subtract).then_inc(lo_ok, 1)
                        if c == 2 * PER and t.group == "A" and not ropes(t, "q"):
                            h = 0 if t.head is None else t.head + 1
                            if t.head is not None:
                                pool.wait_ge(low_ok, blocks_before(t, ST))
                            hold(pool, toep_in, (h + 1) * 16)
                            near = (BAND_TILES - 2) * P
                            nc.gpsimd.tensor_scalar(band[:, near:], toeplitz, 1 / SCALE, None, ALU.mult).then_inc(band_steps, 1)
                            nc.gpsimd.tensor_scalar(band[:, 0:near], toeplitz[:, 0:1].to_broadcast([P, near]), 1 / SCALE, None,
                                                    ALU.mult).then_inc(band_steps, 1)
                            hold(pool, band_steps, h * 3 + 2)
                            nc.gpsimd.memset(band[CHUNK:P, 0:CHUNK], NEG).then_inc(band_steps, 1)
                            hold(pool, band_steps, h * 3 + 3)
                            nc.gpsimd.memset(band[0:CHUNK, BAND_TILES * P - CHUNK:], NEG).then_inc(band_ok, 1)
                all_turns(pool, run)

            @block.tensor
            def _(pe):
                def scores(t, b):
                    n, first = width(t, b)
                    pe.wait_ge(exp_ok, blocks_before(t, b) + 1)
                    if b == 0:
                        pe.wait_ge(part_lo, t.parts0 if t.group == "A" else t.parts0 - 1)
                    if b == ST // 2 and t.group == "B":
                        pe.wait_ge(part_lo, t.parts0)
                    for c0 in range(0, n * P, COL):
                        c1 = min(c0 + COL, n * P)
                        at = slice(first * P + c0, first * P + c1)
                        last = matmul3(nc, s_ps[:, c0:c1], q_hi[:, bass.ts(b, P)], q_lo[:, bass.ts(b, P)], k_hi[:, at], k_lo[:, at],
                                       True, True)
                    last.then_inc(s_ok, 1)

                def turn_round(t, rnd, src_tiles):
                    wait(pe, turned_lo, rnd)
                    for j, i in enumerate(src_tiles):
                        last = nc.tensor.transpose(t_ps[:, bass.ts(j, P)], prob[:, bass.ts(i, P)], m.ident)
                    last.then_inc(turned, 1)

                def pv(t, b):
                    n, first = width(t, b)
                    rounds, before = block_rounds(b)
                    pe.wait_ge(turned_lo, t.round0 + (before + rounds))
                    pe.wait_ge(y_ok, blocks_before(t, b) + 1)
                    for i in range(n):
                        v_at, p_at = bass.ts(first + i, P), bass.ts(i, P)
                        last = matmul3(nc, o_ps[:, 0:P], v_hi[:, v_at], v_lo[:, v_at], pt_hi[:, p_at], pt_lo[:, p_at],
                                       i == 0, i == n - 1)
                    last.then_inc(pv_ok, 1)

                def run(t, more):
                    for pos in positions(t):
                        if t.head is not None and pos < ATTEND:
                            if pos in PV_AT:
                                pv(t, PV_AT.index(pos))
                            for r in range(2):
                                if pos - r in TURN_AT:
                                    b = TURN_AT.index(pos - r)
                                    rounds, before = block_rounds(b)
                                    if r < rounds:
                                        if r == 0:
                                            pe.wait_ge(norm_ok, blocks_before(t, b + 1))
                                        turn_round(t, t.round0 + (before + r), range(4 * r, min(4 * r + 4, width(t, b)[0])))
                            if pos in QK_AT:
                                scores(t, QK_AT.index(pos))
                        if has(t, "v"):
                            for r in range(V_ROUNDS):
                                if pos == role_at(t, "v") + 3 + 2 * r:
                                    if r == 0:
                                        pe.wait_ge(v_read, 1 if t.head is None else t.head + 2)
                                    turn_round(t, t.round0 + ((0 if t.head is None else HEAD_ROUNDS) + r), range(4 * r, 4 * r + 4))
                        if pos >= KT * len(t.tiles):
                            continue
                        tile, k = pos // KT, pos % KT
                        if k == 0 and t.head is not None:
                            if tile == 0:
                                pe.wait_ge(v_read, t.head + 1 if t.group == "A" else H_A + 1)
                                if t.group == "B":
                                    pe.wait_ge(rope_read, t.reads0)
                            elif tile == 1:
                                pe.wait_ge(gate_ok, t.head + 1)
                        if k == 0 and tile >= 2:
                            if ropes(t, "q"):
                                pe.wait_ge(rope_read, t.reads0 + 2 * (tile - 1))
                            else:
                                pe.wait_ge(part_lo, t.parts0 + 2 * (tile - 1))
                        c = pos // KC
                        if pos % KC == 0:
                            pe.wait_ge(lo_ok, t.chunk0 + (c + 1))
                        for h in range(2):
                            at = slice(h * COL, (h + 1) * COL)
                            last = matmul3(nc, proj[tile % 2][:, at], w_hi[:, c % SLOTS, pos % KC, :], w_lo[:, c % SLOTS, pos % KC, :],
                                           m.x_hi[:, k, at], m.x_lo[:, k, at], k == 0, k == KT - 1)
                        if pos % KC == KC - 1:
                            last.then_inc(chunk_used, 1)
                pe.sem_inc(pv_ok, 1)
                all_turns(pe, run)

            def part(role, h):
                at = slice(h * COL, (h + 1) * COL)
                return (q_hi[:, at], q_lo[:, at]) if role == "q" else (k_hi[:, at], k_lo[:, at])

            ROPE = {"q": [(26, 27, 28), (30, 30, 31)], "k": [(33, 34, 35), (36, 37, 38)]}
            PLAIN = {"q": [(27, 28), (27, 28)], "k": [(33, 34), (33, 34)]}

            @block.scalar
            def _(act):
                def split_hi(t, c):
                    act.wait_ge(raw_in[c % SLOTS], (t.raw0 + (c // SLOTS + 1)) * 16)
                    wait(act, chunk_used, t.chunk0 + (c - SLOTS + 1))
                    nc.scalar.copy(w_hi[:, c % SLOTS, :, :], w_raw[:, c % SLOTS, :, :]).then_inc(hi_ok, 1)

                def turned_part(t, rnd, dst_hi, w):
                    act.wait_ge(turned, rnd + 1)
                    nc.scalar.copy(dst_hi, t_ps[:, 0:w]).then_inc(turned_hi, 1)

                def run(t, more):
                    for pos in positions(t):
                        if pos == 1 and t.head is not None:
                            act.wait_ge(y_out, (t.head + 1) * 16)
                            hold(act, chunk_used, t.chunk0)
                            col = COL_GA + t.head if t.group == "A" else t.head + (COL_GB - H_A)
                            nc.scalar.activation(gate[:], proj[1][:], ACT.Exp, bias=m.b_neg[:, bass.ds(col, 1)], scale=-1.0) \
                                .then_inc(gate_exp, 1)
                        if t.head is not None and pos < ATTEND:
                            for r in range(2):
                                if pos - r in TURN_AT:
                                    b = TURN_AT.index(pos - r)
                                    rounds, before = block_rounds(b)
                                    if r < rounds:
                                        if r == 0:
                                            act.wait_ge(pv_ok, blocks_before(t, b) + 1)
                                        w = min(4, width(t, b)[0] - 4 * r) * P
                                        turned_part(t, t.round0 + (before + r), pt_hi[:, 4 * r * P:4 * r * P + w], w)
                            if pos in EXP_AT:
                                b = EXP_AT.index(pos)
                                w = width(t, b)[0] * P
                                act.wait_ge(low_ok, blocks_before(t, b + 1))
                                wait(act, turned, t.round0 + block_rounds(b)[1])
                                nc.scalar.activation(prob[:, 0:w], s_ps[:, 0:w], ACT.Exp, bias=low[:, b:b + 1], scale=-1.0,
                                                     accum_out=total[:, b:b + 1]).then_inc(exp_ok, 1)
                        for role in "qk":
                            if not has(t, role):
                                continue
                            col = [c for r, c, _ in t.tiles if r == role][0]
                            bias = m.b_col[:, bass.ds(col, 1)]
                            done = role_at(t, role)
                            for h in range(2):
                                at = slice(h * COL, (h + 1) * COL)
                                number = 2 * (role == "k") + h
                                if ropes(t, role):
                                    read, _, split = ROPE[role][h]
                                    if pos == read:
                                        act.wait_ge(part_lo, t.parts0 + number)
                                        hold(act, chunk_used, t.chunk0 + done // KC)
                                        nc.scalar.activation(plain, proj[done // KT - 1][:, at], ACT.Identity, bias=bias)
                                        for lo, hi in ((0, 64), (64, 0)):
                                            last = nc.scalar.activation(swapped[lo:lo + 64, :], proj[done // KT - 1][hi:hi + 64, at],
                                                                        ACT.Identity, bias=bias[hi:hi + 64, :])
                                        last.then_inc(rope_read, 1)
                                    if pos == split:
                                        act.wait_ge(roped, t.reads0 + (number + 1))
                                        wait(act, s_ok, blocks_before(t, ST))
                                        nc.scalar.copy(part(role, h)[0], plain).then_inc(part_hi, 1)
                                elif pos == PLAIN[role][h][0]:
                                    if t.head is not None:
                                        act.wait_ge(s_ok, blocks_before(t, ST))
                                    hold(act, chunk_used, t.chunk0 + done // KC)
                                    nc.scalar.activation(part(role, h)[0], proj[done // KT - 1][:, at], ACT.Identity, bias=bias) \
                                        .then_inc(part_hi, 1)
                        if has(t, "v"):
                            done = role_at(t, "v")
                            r0 = t.round0 + (0 if t.head is None else HEAD_ROUNDS)
                            if pos == done + 1:
                                wait(act, turned, r0)
                                hold(act, chunk_used, t.chunk0 + done // KC)
                                nc.scalar.activation(prob[:], proj[0][:], ACT.Identity, bias=m.b_col[:, bass.ds(t.tiles[2][1], 1)]) \
                                    .then_inc(v_read, 1)
                            for r in range(V_ROUNDS):
                                if pos == done + 3 + 2 * r:
                                    if r == 0 and t.head is not None:
                                        act.wait_ge(pv_ok, blocks_before(t, ST) + 1)
                                    turned_part(t, r0 + r, v_hi[:, bass.ts(r, COL)], COL)
                        if pos % KC == 1 and pos < KT * len(t.tiles):
                            c = pos // KC + LEAD
                            if c < PER * len(t.tiles) or more:
                                split_hi(t, c)
                    if t.head is not None:
                        act.wait_ge(y_ok, blocks_before(t, ST) + 1)
                        act.dma_start(io["y"][bass.ds(t.head, 1), :, :].rearrange("h p s -> p (h s)"), gate[:]).then_inc(y_out, 16)
                act.sem_inc(exp_ok, 1)
                act.sem_inc(y_out, 16)
                first = turn_a(0, peeled=True)
                for c in range(LEAD):
                    split_hi(first, c)
                all_turns(act, run)
                act.wait_ge(y_out, (H_A + H_B + 1) * 16)

            @block.vector
            def _(dve):
                def turned_part(rnd, dst_hi, dst_lo, w):
                    dve.wait_ge(turned_hi, rnd + 1)
                    nc.vector.tensor_tensor(dst_lo, t_ps[:, 0:w], f(dst_hi), ALU.subtract).then_inc(turned_lo, 1)

                def run(t, more):
                    for pos in positions(t):
                        if pos == 1 and t.head is not None:
                            dve.wait_ge(gate_exp, t.head + 1)
                            nc.vector.tensor_scalar(gate[:], gate[:], 1.0, None, ALU.add).then_inc(gate_steps, 1)
                            dve.wait_ge(gate_steps, t.head * 2 + 1)
                            nc.vector.reciprocal(gate[:], gate[:]).then_inc(gate_steps, 1)
                            dve.wait_ge(gate_steps, t.head * 2 + 2)
                            col = COL_GA + t.head if t.group == "A" else t.head + (COL_GB - H_A)
                            nc.vector.scalar_tensor_tensor(gate[:], proj[1][:], m.b_col[:, bass.ds(col, 1)], gate[:], ALU.add, ALU.mult) \
                                .then_inc(gate_ok, 1)
                        if t.head is not None and pos < ATTEND:
                            if pos in PV_AT:
                                b = PV_AT.index(pos)
                                dve.wait_ge(pv_ok, blocks_before(t, b + 1) + 1)
                                dve.wait_ge(gate_ok, t.head + 1)
                                nc.vector.tensor_tensor(gate[:, bass.ts(b, P)], o_ps[:, 0:P], gate[:, bass.ts(b, P)], ALU.mult) \
                                    .then_inc(y_ok, 1)
                            for r in range(2):
                                if pos - r in TURN_AT:
                                    b = TURN_AT.index(pos - r)
                                    rounds, before = block_rounds(b)
                                    if r < rounds:
                                        w = min(4, width(t, b)[0] - 4 * r) * P
                                        at = slice(4 * r * P, 4 * r * P + w)
                                        turned_part(t.round0 + (before + r), pt_hi[:, at], pt_lo[:, at], w)
                            if pos in QK_AT:
                                b = QK_AT.index(pos)
                                w = width(t, b)[0] * P
                                if t.group == "A":
                                    bias = band[:, BAND_TILES * P - w:]
                                    if b == 0:
                                        dve.wait_ge(band_ok, t.head + 1)
                                else:
                                    bias = m.mask[:, MASK_AT[b]:MASK_AT[b] + w]
                                hold(dve, s_ok, blocks_before(t, b + 1))
                                nc.vector.tensor_tensor_reduce(out=s_ps[:, 0:w], in0=s_ps[:, 0:w], in1=bias, scale=-SCALE, scalar=3e38,
                                                               op0=ALU.add, op1=ALU.min, accum_out=low[:, b:b + 1]).then_inc(low_ok, 1)
                            if pos in NORM_AT:
                                b = NORM_AT.index(pos)
                                w = width(t, b)[0] * P
                                dve.wait_ge(exp_ok, blocks_before(t, b + 1) + 1)
                                nc.vector.reciprocal(inv[:, b:b + 1], total[:, b:b + 1]).then_inc(inv_ok, 1)
                                dve.wait_ge(inv_ok, blocks_before(t, b + 1))
                                nc.vector.tensor_scalar(prob[:, 0:w], prob[:, 0:w], inv[:, b:b + 1], None, ALU.mult).then_inc(norm_ok, 1)
                        for role in "qk":
                            if not has(t, role):
                                continue
                            col = [c for r, c, _ in t.tiles if r == role][0]
                            done = role_at(t, role)
                            for h in range(2):
                                at = slice(h * COL, (h + 1) * COL)
                                number = 2 * (role == "k") + h
                                hi, lo = part(role, h)
                                if ropes(t, role):
                                    _, rotate, split = ROPE[role][h]
                                    if pos == rotate:
                                        dve.wait_ge(tab_in, 16)
                                        dve.wait_ge(rope_read, t.reads0 + (number + 1))
                                        nc.vector.tensor_tensor(plain, plain, tab[:, 1, at], ALU.mult).then_inc(rope_steps, 1)
                                        nc.vector.tensor_tensor(swapped, swapped, tab[:, 0, at], ALU.mult).then_inc(rope_steps, 1)
                                        dve.wait_ge(rope_steps, t.reads0 * 2 + (2 * number + 2))
                                        nc.vector.tensor_tensor(plain, plain, swapped, ALU.add).then_inc(roped, 1)
                                    if pos == split:
                                        dve.wait_ge(part_hi, t.parts0 + (number + 1))
                                        nc.vector.tensor_tensor(lo, plain, f(hi), ALU.subtract).then_inc(part_lo, 1)
                                elif pos == PLAIN[role][h][1]:
                                    dve.wait_ge(part_hi, t.parts0 + (number + 1))
                                    nc.vector.scalar_tensor_tensor(lo, proj[done // KT - 1][:, at], m.b_col[:, bass.ds(col, 1)], f(hi),
                                                                   ALU.add, ALU.subtract).then_inc(part_lo, 1)
                        if has(t, "v"):
                            r0 = t.round0 + (0 if t.head is None else HEAD_ROUNDS)
                            for r in range(V_ROUNDS):
                                if pos == role_at(t, "v") + 3 + 2 * r:
                                    turned_part(r0 + r, v_hi[:, bass.ts(r, COL)], v_lo[:, bass.ts(r, COL)], COL)
                dve.sem_inc(y_ok, 1)
                all_turns(dve, run)


class Mem:
    pass


def out_block(nc, sem, m, io):
    with ExitStack() as ctx:
        st = Store(nc, ctx)
        RAW, SLOTS, STAGES = 2, 4, 4
        w_raw = st.sb("ow_raw", [P, RAW, COL])
        w_hi = st.sb("ow_hi", [P, SLOTS, COL], F32R)
        w_lo = st.sb("ow_lo", [P, SLOTS, COL], F32R)
        stage = st.sb("stage", [P, STAGES, COL])
        NS = HALF // P
        row = st.sb("row", [P, NS, D_MODEL])
        ln_g, ln_b = st.sb("ln_g", [P, D_MODEL]), st.sb("ln_b", [P, D_MODEL])
        stats = st.sb("stats", [P, NS, D_MODEL // COL, 6])
        mean_var = st.sb("mean_var", [P, NS, 2])
        dev = st.sb("dev", [P, NS, 3])
        bank = [st.ps(f"o_bank{n}", [P, COL]) for n in range(2 * NS)]
        y_hi, y_lo = m.x_hi, m.x_lo

        raw_in = [sem(f"ow_in{n}") for n in range(RAW)]
        stage_in = [sem(f"stage_in{n}") for n in range(STAGES)]
        hi_ok, lo_ok, chunk_used, out_done, bank_free = (
            sem("ow_hi_ok"), sem("ow_lo_ok"), sem("ow_used"), sem("out_done"), sem("o_bank_free"))
        y_hi_ok, stage_used = sem("y_hi_ok"), sem("stage_used")
        term_in = [sem(f"term_in{s}") for s in range(NS)]
        row_out = [sem(f"row_out{s}") for s in range(NS)]
        ln_in, ln_steps, root_in, root_ok, ln_ok = sem("ln_in"), sem("ln_steps"), sem("root_in"), sem("root_ok"), sem("ln_ok")

        CH = 2 * KT
        y_item = lambda half, k: k if half == 0 else KT + 2 * k + 1
        x_item = lambda half, j: KT + 2 * j if half == 0 else 3 * KT + j
        w_rows = io["w_out"].rearrange("(k p) n -> k p n", p=P)
        rows_of = lambda t, half, s: t.rearrange("(h s p) n -> h s p n", h=2, p=P)[half, s]

        with nc.Block() as block:
            @block.sync
            def _(sp):
                def item(n, src):
                    if n >= STAGES:
                        sp.wait_ge(stage_used, n - STAGES + 1)
                    sp.dma_start(stage[:, n % STAGES, :], src).then_inc(stage_in[n % STAGES], 16)

                for it in range(4):
                    half, pair = it // 2, it % 2
                    for k in range(KT):
                        if pair == 1:
                            s, c = k // 4, k % 4
                            item(x_item(half, k), rows_of(io["x"], half, s)[:, bass.ts(c, COL)])
                        if it < 2:
                            item(y_item(it, k), io["y"][k, :, it * HALF:(it + 1) * HALF])
                        for cb in range(2):
                            n = it * CH + 2 * k + cb
                            if n >= RAW:
                                sp.wait_ge(lo_ok, n - RAW + 1)
                            sp.dma_start(w_raw[:, n % RAW, :], w_rows[k, :, pair * 2 * COL + cb * COL:pair * 2 * COL + (cb + 1) * COL]) \
                                .then_inc(raw_in[n % RAW], 16)
                        if it == 0 and 4 <= k < 4 + NS:
                            sp.dma_start(row[:, k - 4, :], rows_of(io["gate_term"], 0, k - 4)).then_inc(term_in[k - 4], 16)
                        if it == 1 and k == 0:
                            sp.dma_start(ln_g[:], io["ln_g"].partition_broadcast(P)).then_inc(ln_in, 16)
                            sp.dma_start(ln_b[:], io["ln_b"].partition_broadcast(P)).then_inc(ln_in, 16)
                        if it == 2 and 9 <= k < 9 + NS:
                            sp.wait_ge(ln_ok, k - 9 + 1)
                            sp.dma_start(rows_of(io["out"], 0, k - 9), row[:, k - 9, :]).then_inc(row_out[k - 9], 16)
                        if it == 2 and 11 <= k < 11 + NS:
                            sp.wait_ge(row_out[k - 11], 16)
                            sp.dma_start(row[:, k - 11, :], rows_of(io["gate_term"], 1, k - 11)).then_inc(term_in[k - 11], 16)
                for s in range(NS):
                    sp.wait_ge(ln_ok, NS + s + 1)
                    sp.dma_start(rows_of(io["out"], 1, s), row[:, s, :]).then_inc(row_out[s], 16)
                for s in range(NS):
                    sp.wait_ge(row_out[s], 32)

            @block.gpsimd
            def _(pool):
                with pool.Fori(0, 4 * CH // SLOTS) as i:
                    for c in range(SLOTS):
                        pool.wait_ge(hi_ok, i * SLOTS + c + 1)
                        nc.gpsimd.tensor_tensor(w_lo[:, c, :], w_raw[:, c % RAW, :], f(w_hi[:, c, :]), ALU.subtract).then_inc(lo_ok, 1)

            @block.tensor
            def _(pe):
                for half in range(2):
                    with pe.Fori(2 * half, 2 * half + 2) as it:
                        for k in range(KT):
                            pe.wait_ge(stage_used, y_item(half, k) + 1)
                            for cb in range(2):
                                slot = (2 * k + cb) % SLOTS
                                pe.wait_ge(lo_ok, it * CH + (2 * k + cb + 1))
                                for s in range(NS):
                                    at = bass.ts(half * NS + s, P)
                                    if k == 0:
                                        pe.wait_ge(bank_free, it * 2 * NS + (cb * NS + s + 1))
                                    last = matmul3(nc, bank[cb * NS + s][:], y_hi[:, k, at], y_lo[:, k, at], w_hi[:, slot, :],
                                                   w_lo[:, slot, :], k == 0, k == KT - 1)
                                    if k == KT - 1:
                                        last.then_inc(out_done, 1)
                                if k < KT - 1:
                                    last.then_inc(chunk_used, 1)

            @block.scalar
            def _(act):
                def split_hi(it, c):
                    n = it * CH + c
                    act.wait_ge(raw_in[n % RAW], 16 * (n // RAW + 1))
                    old = n - SLOTS
                    if old >= 0:
                        o_it, o_c = old // CH, old % CH
                        if o_c >= CH - 2:
                            act.wait_ge(out_done, o_it * 2 * NS + (o_c - CH + 3) * NS)
                        else:
                            act.wait_ge(chunk_used, o_it * (CH - 2) + o_c + 1)
                    nc.scalar.copy(w_hi[:, n % SLOTS, :], w_raw[:, n % RAW, :]).then_inc(hi_ok, 1)

                def root(half, s):
                    act.wait_ge(root_in, half * NS + s + 1)
                    nc.scalar.activation(dev[:, s, 1:2], dev[:, s, 0:1], ACT.Sqrt).then_inc(root_ok, 1)

                for it in range(4):
                    for k in range(KT):
                        if it < 2:
                            n = y_item(it, k)
                            act.wait_ge(stage_in[n % STAGES], 16 * (n // STAGES + 1))
                            nc.scalar.copy(y_hi[:, k, it * HALF:(it + 1) * HALF], stage[:, n % STAGES, :]).then_inc(y_hi_ok, 1)
                        for cb in range(2):
                            split_hi(it, 2 * k + cb)
                        if it == 2 and k in (1, 2, 4, 5):
                            root(0, (1, 2, 4, 5).index(k))
                for s in range(NS):
                    root(1, s)

            @block.vector
            def _(dve):
                dve.sem_inc(bank_free, 2 * NS)
                ch = Chain(dve, ln_steps)

                def split_y(half, k):
                    n = y_item(half, k)
                    dve.wait_ge(y_hi_ok, half * KT + k + 1)
                    at = slice(half * HALF, (half + 1) * HALF)
                    nc.vector.tensor_tensor(y_lo[:, k, at], stage[:, n % STAGES, :], f(y_hi[:, k, at]), ALU.subtract) \
                        .then_inc(stage_used, 1)

                def add_x(half, j):
                    n = x_item(half, j)
                    at = row[:, j // 4, bass.ts(j % 4, COL)]
                    dve.wait_ge(stage_in[n % STAGES], 16 * (n // STAGES + 1))
                    nc.vector.scalar_tensor_tensor(at, stage[:, n % STAGES, :], ALPHA, at, ALU.mult, ALU.add).then_inc(stage_used, 1)

                def add_y(it):
                    half, pair = it // 2, it % 2
                    for n in range(2 * NS):
                        cb, s = n // NS, n % NS
                        at = row[:, s, bass.ts(2 * pair + cb, COL)]
                        dve.wait_ge(out_done, it * 2 * NS + n + 1)
                        dve.wait_ge(term_in[s], 16 * (half + 1))
                        nc.vector.tensor_tensor(at, bank[n][:], at, ALU.add).then_inc(bank_free, 1)
                    dve.wait_ge(bank_free, (it + 2) * 2 * NS)

                def statistics(half, s):
                    for c in range(D_MODEL // COL):
                        ch.step(nc.vector.bn_stats(stats[:, s, c, :], row[:, s, bass.ts(c, COL)]))
                    ch.wait()
                    ch.link(nc.vector.bn_aggr(mean_var[:, s, :], stats[:, s, :, :]))
                    nc.vector.tensor_scalar(dev[:, s, 0:1], mean_var[:, s, 1:2], LN_EPS, None, ALU.add).then_inc(root_in, 1)

                def normalise(half, s):
                    dve.wait_ge(root_ok, half * NS + s + 1)
                    ch.link(nc.vector.reciprocal(dev[:, s, 2:3], dev[:, s, 1:2]))
                    ch.link(nc.vector.tensor_scalar(row[:, s, :], row[:, s, :], mean_var[:, s, 0:1], dev[:, s, 2:3], ALU.subtract, ALU.mult))
                    ch.link(nc.vector.tensor_tensor(row[:, s, :], row[:, s, :], ln_g[:], ALU.mult))
                    nc.vector.tensor_tensor(row[:, s, :], row[:, s, :], ln_b[:], ALU.add).then_inc(ln_ok, 1)

                def norm_half(half):
                    dve.wait_ge(ln_in, 32)
                    for s in range(NS + 1):
                        if s < NS:
                            statistics(half, s)
                        if s:
                            normalise(half, s - 1)

                for k in range(KT):
                    split_y(0, k)
                add_y(0)
                for k in range(KT):
                    add_x(0, k)
                    split_y(1, k)
                dve.wait_ge(stage_used, y_item(1, KT - 1) + 1)
                add_y(1)
                norm_half(0)
                add_y(2)
                for j in range(KT):
                    add_x(1, j)
                dve.wait_ge(stage_used, x_item(1, KT - 1) + 1)
                add_y(3)
                norm_half(1)


def hybrid_layer_kernel(nc, io):
    m = Mem()
    with ExitStack() as ctx:
        def sem(name):
            return ctx.enter_context(nc.semaphore(name))
        top = Store(nc, ctx)
        m.x_hi = top.sb("x_hi", [P, KT, SEQ], F32R)[:]
        m.x_lo = top.sb("x_lo", [P, KT, SEQ], F32R)[:]
        with ExitStack() as until_out:
            st = Store(nc, until_out)
            m.ident = st.sb("ident", [P, P])[:]
            m.b_col = st.sb("b_col", [P, BIAS_COLS])[:]
            m.b_neg = st.sb("b_neg", [P, BIAS_COLS])[:]
            m.kw_bias = st.sb("kw_bias", [KW, 1])[:]
            tab_or_mask = st.sb("tab_or_mask", [P, max(2 * SEQ, MASK_COLS // 2)])[:]
            m.cos_i, m.sin_i = tab_or_mask[:, 0:SEQ], tab_or_mask[:, SEQ:2 * SEQ]
            m.mask = tab_or_mask[:, 0:MASK_COLS // 2].bitcast(BF16)
            with ExitStack() as until_picked:
                m.scores = Store(nc, until_picked).sb("scores", [P, SCORE_COLS])[:]
                load_block(nc, sem, m, io)
                index_block(nc, sem, m, io)
                gate_block(nc, sem, m, io)
            heads_block(nc, sem, m, io)
        out_block(nc, sem, m, io)


def rotary_constants():
    c = np.zeros((P, 4), np.float32)
    for n, dim in enumerate((D_IDX, HEAD_DIM)):
        inv = np.float32(ROPE_THETA) ** (-np.arange(0, dim, 2, dtype=np.float32) / np.float32(dim))
        c[:, n] = inv[np.arange(P) % (dim // 2)]
        c[:, 2 + n] = np.where(np.arange(P) % dim < dim // 2, -1, 1)
    return c


def kernel(x, p, positions, w_in, b_in, rel_bias, w_out, w_ple, w_ple_gate, b_ple_gate, ln_g, ln_b):
    import concourse.bacc as bacc
    from concourse.bass_utils import run_bass_kernel_spmd

    arrays = {
        "x": x.reshape(SEQ, D_MODEL), "p": p.reshape(SEQ, D_PLE), "positions": positions.reshape(SEQ),
        "w_in": w_in.reshape(D_MODEL, D_IN), "b_in": b_in.reshape(D_IN), "rel_bias": rel_bias.reshape(H_A, N_REL),
        "w_out": w_out.reshape(D_MODEL, D_MODEL), "w_ple": w_ple.reshape(D_PLE, D_MODEL),
        "w_pg": w_ple_gate.reshape(D_MODEL, D_MODEL), "b_pg": b_ple_gate.reshape(D_MODEL),
        "ln_g": ln_g.reshape(D_MODEL), "ln_b": ln_b.reshape(D_MODEL), "rotary": rotary_constants(),
    }
    nc = bacc.Bacc("TRN2", target_bir_lowering=False, num_devices=1)
    io, feeds = {}, {}
    for name, a in arrays.items():
        a = np.ascontiguousarray(a)
        feeds[f"in_{name}"] = a
        io[name] = nc.dram_tensor(f"in_{name}", a.shape, mybir.dt.from_np(a.dtype), kind="ExternalInput").ap()
    for name, shape in {"head_tab": (2, P, SEQ), "gate_term": (SEQ, D_MODEL), "rel_pad": (H_A, 3 * P), "rel_skew": (H_A, P, 2 * P),
                        "y": (H_A + H_B, HEAD_DIM, SEQ)}.items():
        io[name] = nc.dram_tensor(f"scratch_{name}", shape, F32, kind="Internal").ap()
    io["out"] = nc.dram_tensor("out_dram", (SEQ, D_MODEL), F32, kind="ExternalOutput").ap()
    hybrid_layer_kernel(nc, io)
    result = run_bass_kernel_spmd(nc, [feeds], core_ids=[0])
    return result.results[0]["out_dram"].reshape(x.shape)
```

```python
from contextlib import ExitStack

import numpy as np

import concourse.bass as bass
from concourse import mybir

F32 = mybir.dt.float32
F32R = mybir.dt.float32r
BF16 = mybir.dt.bfloat16
I32 = mybir.dt.int32
ALU = mybir.AluOpType
ACT = mybir.ActivationFunctionType

P = 128
SEQ = 1024
D_MODEL = 2048
D_IN = 6984
D_PLE = 256
CHUNK = 64
HEAD_DIM = 128
H_A = 8
H_B = 8
H_IDX = 8
D_IDX = 64
TOPK = 256
REL_CLIP = 128
N_REL = 2 * REL_CLIP + 1
ROPE_THETA = 10000.0
LN_EPS = 1e-5
ALPHA = 2.0 ** 0.25
NEG = -1e30
TAKEN = -3e38

KT = D_MODEL // P
ST = SEQ // P
HALF = SEQ // 2
COL = 512
BIAS_COLS = D_IN // P
COL_QA, COL_KA, COL_VA, COL_GA, COL_QB, COL_KB, COL_VB, COL_GB, COL_QI = 0, 8, 16, 24, 32, 40, 41, 42, 50
COL_KW = BIAS_COLS * P
KW = D_IDX + H_IDX
FIRST_PICKED = TOPK // P
BAND_TILES = 5
MASK_AT = [P, 0] + [2 * P + sum((j + 1) * P for j in range(FIRST_PICKED, b)) for b in range(FIRST_PICKED, ST)]
MASK_COLS = MASK_AT[-1] + SEQ
SCORE_AT = [None, None] + [m - 2 * P for m in MASK_AT[2:]]
SCORE_COLS = MASK_COLS - 2 * P

TWO_PI_1 = 6.28125
TWO_PI_2 = float(np.float32(round((2 * np.pi - TWO_PI_1) * 2 ** 20) / 2 ** 20))
TWO_PI_3 = float(np.float32(2 * np.pi - TWO_PI_1 - TWO_PI_2))
ROUND = 1.5 * 2 ** 23
PI_BELOW = 3.1415925


def hold(eng, sem, value):
    eng.wait_ge(sem, value)
    eng.nop(nofuse=True)


class Store:

    def __init__(self, nc, ctx):
        self.nc, self.ctx = nc, ctx

    def sb(self, name, shape, dt=F32):
        return self.ctx.enter_context(self.nc.sbuf_tensor(name, shape, dt))

    def ps(self, name, shape):
        return self.ctx.enter_context(self.nc.psum_tensor(name, shape, F32))


class Chain:

    def __init__(self, eng, sem):
        self.eng, self.sem, self.n, self.base = eng, sem, 0, 0

    def step(self, ins):
        ins.then_inc(self.sem, 1)
        self.n += 1

    def wait(self):
        hold(self.eng, self.sem, self.base + self.n)

    def link(self, ins):
        self.step(ins)
        self.wait()

    def enter(self, i, per):
        self.start, self.per, self.base, self.n = self.base + self.n, per, self.base + self.n + i * per, 0

    def leave(self, count):
        assert self.n == self.per, self.n
        self.base, self.n = self.start + count * self.per, 0


def f(ap):
    return ap.bitcast(F32)


def matmul3(nc, out, l_hi, l_lo, r_hi, r_lo, start, stop, **kw):
    nc.tensor.matmul(out, l_hi, r_hi, start=start, stop=False, **kw)
    nc.tensor.matmul(out, l_hi, r_lo, start=False, stop=False, **kw)
    return nc.tensor.matmul(out, l_lo, r_hi, start=False, stop=stop, **kw)


def rotary_argument(nc, step, ang, turns, arg, quarter, sign, before=None):
    step(nc.vector.tensor_scalar(turns, ang, 1.0 / (2 * np.pi), quarter, ALU.mult, ALU.add))
    step(nc.vector.tensor_scalar(turns, turns, ROUND, -ROUND, ALU.add, ALU.add))
    if before is not None:
        before()
    step(nc.vector.scalar_tensor_tensor(arg, turns, -TWO_PI_1, ang, ALU.mult, ALU.add))
    step(nc.vector.scalar_tensor_tensor(arg, turns, -TWO_PI_2, arg, ALU.mult, ALU.add))
    step(nc.vector.scalar_tensor_tensor(arg, turns, -TWO_PI_3, arg, ALU.mult, ALU.add))
    if quarter:
        step(nc.vector.tensor_scalar(arg, arg, 0.5 * np.pi, None, ALU.add))
    else:
        step(nc.vector.tensor_scalar(arg, arg, sign, None, ALU.mult))
    return nc.vector.tensor_scalar(arg, arg, PI_BELOW, -PI_BELOW, ALU.min, ALU.max)


def load_index_phase(nc, block, sem, m, io):
    with ExitStack() as ctx:
        st = Store(nc, ctx)
        RAW, PART = 2, 4
        w_raw = st.sb("iw_raw", [P, RAW, 4, P])
        w_hi = st.sb("iw_hi", [P, PART, 4, P], F32R)
        w_lo = st.sb("iw_lo", [P, PART, 4, P], F32R)
        ki_hi = st.sb("ki_hi", [P, SEQ], F32R)
        ki_lo = st.sb("ki_lo", [P, SEQ], F32R)
        w_idx = st.sb("w_idx", [P, ST, H_IDX])
        b_row = st.sb("b_row", [BIAS_COLS, P])
        rel = st.sb("rel", [H_A, 3 * P])
        with ExitStack() as rows:
            x_row = Store(nc, rows).sb("x_row", [P, 4, D_MODEL // 2])
        qi = [st.sb("qi_even", [P, SEQ], F32R), st.sb("qi_odd", [P, SEQ], F32R)]
        plain = st.sb("i_plain", [P, 2, COL])
        swapped = st.sb("i_swapped", [P, 2, COL])
        pos, ang, turns, rest = (m.scores[:, n * SEQ:(n + 1) * SEQ] for n in range(4))
        pos_i = rest.bitcast(I32)
        proj = [st.ps(f"i_proj{n}", [P, 2, COL]) for n in range(2)]
        dots = [st.ps(f"i_dots{n}", [P, 2, COL]) for n in range(2)]
        x_ps = [dots[g // 2][:, g % 2, :].rearrange("p (k q) -> p k q", k=4) for g in range(4)]
        b_ps = proj[1][:, 0, 0:BIAS_COLS]
        w_ps = dots[1]

        ident_zero, ident_ok = sem("ident_zero"), sem("ident_ok")
        x_in = [sem(f"x_in{n}") for n in range(4)]
        small_in, b_turned, b_ok = sem("small_in"), sem("b_turned"), sem("b_ok")
        x_turned, x_hi_ok, x_free = sem("x_turned"), sem("x_hi_ok"), sem("x_free")
        tab_steps, rest_ok, tab_ok = sem("tab_steps"), sem("rest_ok"), sem("tab_ok")
        rel_in, rel_ok, rel_out = sem("rel_in"), sem("rel_ok"), sem("rel_out")
        raw_in = [sem("iw_in0"), sem("iw_in1")]
        hi_ok, lo_ok, chunk_used = sem("iw_hi_ok"), sem("iw_lo_ok"), sem("iw_used")
        plain_ok, rope_steps, roped, part_hi, part_lo = (
            sem("i_plain_ok"), sem("i_rope_steps"), sem("i_roped"), sem("i_part_hi"), sem("i_part_lo"))
        ki_both, wi_turned, wi_ok = sem("ki_both"), sem("wi_turned"), sem("wi_ok")
        dots_ok, relu_ok, score_ok, corner_ok = sem("dots_ok"), sem("relu_ok"), sem("score_ok"), sem("corner_ok")

        x_rows = io["x"].rearrange("(t p) d -> t p d", p=P)
        tables = [(m.sin_i, 0.0), (m.cos_i, 0.25)]
        TILES = 5
        cols = [(COL_KW, KW)] + [((COL_QI + t) * P, P) for t in range(4)]
        w_rows = io["w_in"].rearrange("(c k p) n -> c p k n", k=4, p=P)
        EARLY = (8, 9)
        steps = [(t, hh, b) for t in range(4) for b in range(FIRST_PICKED, ST) for hh in range(2)]
        PER_TILE = len(steps) // 4
        STEP_AT = list(range(KT - 10, KT - 2)) + [KT - 3, KT - 2, KT - 1, KT - 1]

        LAST_STEPS = 3 * PER_TILE
        assert LAST_STEPS % 6 == 0

        def dots_of(n):
            return dots[n % 2] if n < LAST_STEPS else (dots + [proj[1]])[n % 3]

        m.index_weights_used = chunk_used, 4 * TILES
        m.index_proj_read = plain_ok, 2 * TILES
        m.index_dots_done = dots_ok, len(steps)
        m.index_scored = score_ok, len(steps)

        def parts(t, h):
            at, low, high = slice(h * COL, (h + 1) * COL), slice(0, D_IDX), slice(D_IDX, P)
            if t == 0:
                return [(low, ki_hi[low, at], ki_lo[low, at])]
            return [(low, qi[0][low, at], qi[0][high, at]), (high, qi[1][high, at], qi[1][low, at])]

        @block.sync
        def _(sp):
            def x_tile(s):
                for n in (2 * s, 2 * s + 1):
                    if n >= 4:
                        sp.wait_ge(x_free, 4 + 2 * (n - 4 + 1))
                    sp.dma_start(x_row[:, n % 4, :], x_rows[s][:, bass.ts(n % 2, D_MODEL // 2)]).then_inc(x_in[n % 4], 16)

            def w_chunk(k):
                c0, n = cols[k // 4]
                if k >= RAW:
                    sp.wait_ge(lo_ok, k - RAW + 1)
                sp.dma_start(w_raw[:, k % RAW, :, 0:n], w_rows[k % 4, :, :, c0:c0 + n]).then_inc(raw_in[k % RAW], 16)

            for s in range(ST):
                x_tile(s)
                if s in (2, 4):
                    w_chunk(s - 2)
                    w_chunk(s - 1)
            for k in range(4, 4 * TILES):
                w_chunk(k)
                if k == max(EARLY):
                    sp.wait_ge(part_lo, 2)
                    sp.dma_start(f(ki_hi[D_IDX:P, :]), f(ki_hi[0:D_IDX, :])).then_inc(ki_both, 16)
                    sp.dma_start(f(ki_lo[D_IDX:P, :]), f(ki_lo[0:D_IDX, :])).then_inc(ki_both, 16)
            sp.wait_ge(rel_ok, 1)
            sp.dma_start(io["rel_pad"][:, 0:3 * P - 1], rel[:, 0:3 * P - 1]).then_inc(rel_out, 16)
            sp.wait_ge(rel_out, 16)
            pad = io["rel_pad"]
            sp.dma_start(io["rel_skew"], bass.AP(tensor=pad.tensor, offset=pad.offset + P - 1,
                                                 ap=[[3 * P, H_A], [-1, P], [1, 2 * P]])).then_inc(rel_out, 16)
            sp.wait_ge(rel_out, 32)

        @block.gpsimd
        def _(pool):
            nc.gpsimd.memset(m.ident, 0.0).then_inc(ident_zero, 1)
            pool.wait_ge(ident_zero, 1)
            nc.gpsimd.affine_select(out=m.ident, in_=m.ident, compare_op=ALU.not_equal, fill=1.0, base=0,
                                    pattern=[[-1, P]], channel_multiplier=1).then_inc(ident_ok, 1)
            for k in range(4 * TILES):
                n = cols[k // 4][1]
                pool.wait_ge(hi_ok, k + 1)
                nc.gpsimd.tensor_tensor(w_lo[:, k % PART, :, 0:n], w_raw[:, k % RAW, :, 0:n],
                                        f(w_hi[:, k % PART, :, 0:n]), ALU.subtract).then_inc(lo_ok, 1)

        @block.tensor
        def _(pe):
            pe.wait_ge(ident_ok, 1)
            def turn_group(s, j, x_count, g):
                slot = 2 * j + g // 2
                pe.wait_ge(x_in[slot], x_count)
                pe.wait_ge(x_free, 4 * s + g + 1)
                for k in range(4):
                    last = nc.tensor.transpose(x_ps[g][:, k, :], x_row[:, slot, bass.ts(4 * (g % 2) + k, P)], m.ident)
                last.then_inc(x_turned, 1)

            def product(t, k, h):
                c, n, at = 4 * t + k // 4, cols[t][1], slice(h * COL, (h + 1) * COL)
                return matmul3(nc, proj[t % 2][0:n, h, :], w_hi[:, c % PART, k % 4, 0:n], w_lo[:, c % PART, k % 4, 0:n],
                               m.x_hi[:, k, at], m.x_lo[:, k, at], k == 0, k == KT - 1)

            with pe.Fori(0, ST // 4) as i:
                for j in range(2):
                    for g in range(4):
                        turn_group(i * 2 + j, j, 16 * (i + 1), g)
            for n in range(4 * (ST // 2)):
                s, g = ST // 2 + n // 4, n % 4
                turn_group(s, s % 2, 16 * (s // 2 + 1), g)
                if n == 0:
                    pe.wait_ge(x_free, 4 * (ST // 2 + 1))
                if n % 4 == 0:
                    pe.wait_ge(lo_ok, n // 4 + 1)
                product(0, n, 0)
            pe.wait_ge(small_in, 64)
            nc.tensor.transpose(b_ps, b_row[:], m.ident[0:BIAS_COLS, 0:BIAS_COLS]).then_inc(b_turned, 1)

            def dot(n):
                t, hh, b = steps[n]
                if n == 0:
                    pe.wait_ge(ki_both, 32)
                if n == 1:
                    pe.wait_ge(wi_ok, 1)
                if n >= 2:
                    pe.wait_ge(score_ok, n - 1 if n < LAST_STEPS + 2 else n - 2)
                if n % PER_TILE == 0:
                    pe.wait_ge(part_lo, 2 * t + 3)
                if b == ST // 2 and hh == 0:
                    pe.wait_ge(part_lo, 2 * t + 4)
                rows, at = slice(D_IDX * hh, D_IDX * hh + D_IDX), slice(b * P, b * P + P)
                for c0 in range(0, (b + 1) * P, COL):
                    c1 = min(c0 + COL, (b + 1) * P)
                    out = dots_of(n)[:, c0 // COL, 0:c1 - c0]
                    nc.tensor.matmul(out, qi[hh][:, at], ki_hi[:, c0:c1], start=True, stop=False)
                    last = nc.tensor.matmul(out, qi[hh][rows, at], ki_lo[rows, c0:c1], start=False, stop=True)
                last.then_inc(dots_ok, 1)

            pe.wait_ge(x_free, 4 * (ST + 1))
            for t in range(TILES):
                if t >= 2:
                    pe.wait_ge(plain_ok, 2 * t - 2)
                if t == 1:
                    pe.wait_ge(b_ok, 1)
                for k in range(KT):
                    c = 4 * t + k // 4
                    for n in range(PER_TILE):
                        if t >= 2 and STEP_AT[n] == k:
                            dot((t - 2) * PER_TILE + n)
                    if k % 4 == 0:
                        pe.wait_ge(lo_ok, c + 1)
                    for h in range(2):
                        if t or h:
                            last = product(t, k, h)
                    if k % 4 == 3:
                        last.then_inc(chunk_used, 1)
                if t == 1:
                    pe.wait_ge(plain_ok, 2)
                    for h in range(2):
                        for j in range(4):
                            last = nc.tensor.transpose(w_ps[:, h, bass.ts(j, H_IDX)], plain[D_IDX:KW, h, bass.ts(j, P)],
                                                       m.ident[D_IDX:KW, D_IDX:KW])
                        last.then_inc(wi_turned, 1)
            for n in range(3 * PER_TILE, 4 * PER_TILE):
                dot(n)

        @block.scalar
        def _(act):
            act.dma_start(pos_i, io["positions"].partition_broadcast(P)).then_inc(small_in, 16)
            act.dma_start(m.rotary, io["rotary"]).then_inc(small_in, 16)
            act.dma_start(b_row[:], io["b_in"][0:BIAS_COLS * P].rearrange("(t p) -> t p", p=P)).then_inc(small_in, 16)
            act.dma_start(m.kw_bias, io["b_in"][COL_KW:D_IN].rearrange("(p a) -> p a", a=1)).then_inc(small_in, 16)
            act.dma_start(rel[:, P - 1:3 * P - 1], io["rel_bias"][:, N_REL - 1:0:-1], allow_slow_non_contiguous=True) \
                .then_inc(rel_in, 16)
            def x_parts(first, end):
                with act.Fori(first, end) as i:
                    for j in range(2):
                        s = i * 2 + j
                        for g in range(4):
                            act.wait_ge(x_turned, 4 * s + g + 1)
                            nc.scalar.copy(m.x_hi[:, 4 * g:4 * g + 4, bass.ds(s * P, P)], x_ps[g]).then_inc(x_hi_ok, 1)

            def split_hi(k):
                n = cols[k // 4][1]
                act.wait_ge(raw_in[k % RAW], 16 * (k // RAW + 1))
                if k >= PART:
                    act.wait_ge(chunk_used, k - PART + 1)
                nc.scalar.copy(w_hi[:, k % PART, :, 0:n], w_raw[:, k % RAW, :, 0:n]).then_inc(hi_ok, 1)

            def table(n):
                act.wait_ge(rest_ok, n + 1)
                nc.scalar.activation(tables[n][0], rest, ACT.Sin).then_inc(tab_ok, 1)

            def relu(n):
                _, _, b = steps[n]
                w = (b + 1) * P
                d = dots_of(n)[:].rearrange("p a c -> p (a c)")[:, 0:w]
                act.wait_ge(dots_ok, n + 1)
                nc.scalar.activation(d, d, ACT.Relu, scale=D_IDX ** -0.5).then_inc(relu_ok, 1)

            x_parts(0, ST // 4)
            split_hi(0)
            split_hi(1)
            x_parts(ST // 4, ST // 4 + 1)
            split_hi(2)
            split_hi(3)
            x_parts(ST // 4 + 1, ST // 2)
            for t in range(TILES):
                n = cols[t][1]
                for c in range(4):
                    k = 4 * t + c + 3
                    if c and k < 4 * TILES and k not in EARLY:
                        split_hi(k)
                    if t >= 2:
                        for j in range(PER_TILE):
                            if STEP_AT[j] // 4 == c:
                                relu((t - 2) * PER_TILE + j)
                bias = m.kw_bias if t == 0 else m.b_col[:, COL_QI + t - 1:COL_QI + t]
                act.wait_ge(chunk_used, 4 * (t + 1))
                if t < TILES - 1:
                    split_hi(4 * t + 7)
                if t == 0:
                    table(0)
                    table(1)
                if t == 0:
                    act.wait_ge(small_in, 64)
                if t == 1:
                    act.wait_ge(b_ok, 1)
                for h in range(2):
                    if t == 1:
                        act.wait_ge(part_lo, h + 1)
                        act.wait_ge(wi_turned, h + 1)
                    elif t:
                        act.wait_ge(part_lo, 2 * t - 1 + h)
                    nc.scalar.activation(plain[0:n, h, :], proj[t % 2][0:n, h, :], ACT.Identity, bias=bias[0:n, :])
                    for q in range(n // 32):
                        o = q ^ 1
                        last = nc.scalar.activation(swapped[32 * q:32 * q + 32, h, :], proj[t % 2][32 * o:32 * o + 32, h, :],
                                                    ACT.Identity, bias=bias[32 * o:32 * o + 32, :])
                    last.then_inc(plain_ok, 1)
                if t == 0:
                    for k in EARLY:
                        split_hi(k)
                for h in range(2):
                    act.wait_ge(roped, 2 * t + h + 1)
                    if t >= 2 and h == 0:
                        act.wait_ge(dots_ok, (t - 1) * PER_TILE)
                    for rows, hi, _ in parts(t, h):
                        last = nc.scalar.copy(hi, plain[rows, h, :])
                    last.then_inc(part_hi, 1)
            for n in range(3 * PER_TILE, 4 * PER_TILE):
                relu(n)

        @block.vector
        def _(dve):
            dve.sem_inc(x_free, 4)
            with dve.Fori(0, ST // 2) as i:
                for j in range(2):
                    s = i * 2 + j
                    for g in range(4):
                        dve.wait_ge(x_hi_ok, 4 * s + g + 1)
                        part = (slice(None), slice(4 * g, 4 * g + 4), bass.ds(s * P, P))
                        nc.vector.tensor_tensor(m.x_lo[part], x_ps[g], f(m.x_hi[part]), ALU.subtract).then_inc(x_free, 1)
            dve.wait_ge(b_turned, 1)
            nc.vector.tensor_copy(m.b_col, b_ps).then_inc(b_ok, 1)
            tc = Chain(dve, tab_steps)
            dve.wait_ge(small_in, 64)
            tc.link(nc.vector.tensor_copy(pos, pos_i))

            tc.link(nc.vector.tensor_scalar(ang, pos, m.rotary[:, 0:1], None, ALU.mult))
            for n, (_, quarter) in enumerate(tables):
                rotary_argument(nc, tc.link, ang, turns, rest, quarter, m.rotary[:, 2:3], (lambda: dve.wait_ge(tab_ok, 1)) if n else None) \
                    .then_inc(rest_ok, 1)
            dve.wait_ge(rel_in, 16)
            nc.vector.tensor_copy(rel[:, 0:P - 1], rel[:, P - 1:P].to_broadcast([H_A, P - 1])).then_inc(rel_ok, 1)
            ch = Chain(dve, rope_steps)

            def score(n):
                t, hh, b = steps[n]
                head, w = 2 * t + hh, (b + 1) * P
                at = m.scores[:, SCORE_AT[b]:SCORE_AT[b] + w]
                d = dots_of(n)[:].rearrange("p a c -> p (a c)")[:, 0:w]
                wi = w_idx[:, b, head:head + 1]
                dve.wait_ge(relu_ok, n + 1)
                if head == 0:
                    nc.vector.tensor_scalar(at, d, wi, None, ALU.mult).then_inc(score_ok, 1)
                    return
                dve.wait_ge(score_ok, n if hh else n - PER_TILE + 2)
                nc.vector.scalar_tensor_tensor(at, d, wi, at, ALU.mult, ALU.add).then_inc(score_ok, 1)

            for t in range(TILES):
                r = D_IDX if t == 0 else P
                for h in range(2):
                    at = slice(h * COL, (h + 1) * COL)
                    dve.wait_ge(plain_ok, 2 * t + h + 1)
                    if t == 0 and h == 0:
                        dve.wait_ge(tab_ok, 2)
                    ch.step(nc.vector.tensor_tensor(plain[0:r, h, :], plain[0:r, h, :], m.cos_i[0:r, at], ALU.mult))
                    ch.link(nc.vector.tensor_tensor(swapped[0:r, h, :], swapped[0:r, h, :], m.sin_i[0:r, at], ALU.mult))
                    nc.vector.tensor_tensor(plain[0:r, h, :], plain[0:r, h, :], swapped[0:r, h, :], ALU.add).then_inc(roped, 1)
                    dve.wait_ge(part_hi, 2 * t + h + 1)
                    for rows, hi, lo in parts(t, h):
                        last = nc.vector.tensor_tensor(lo, plain[rows, h, :], f(hi), ALU.subtract)
                    last.then_inc(part_lo, 1)
                if t == 0:
                    dve.wait_ge(wi_turned, 2)
                    nc.vector.tensor_scalar(w_idx[:].rearrange("p (h j) n -> p h (j n)", h=2), w_ps[:, :, 0:4 * H_IDX],
                                            H_IDX ** -0.5, None, ALU.mult).then_inc(wi_ok, 1)
                    dve.wait_ge(wi_ok, 1)
                if t:
                    for n in range((t - 1) * PER_TILE, t * PER_TILE):
                        score(n)
            for b in range(FIRST_PICKED, ST):
                end = SCORE_AT[b] + (b + 1) * P
                dve.wait_ge(score_ok, 4 * PER_TILE)
                nc.vector.memset(m.scores[0:CHUNK, end - CHUNK:end], NEG).then_inc(corner_ok, 1)
            dve.wait_ge(corner_ok, ST - FIRST_PICKED)


def gate_phase(nc, block, sem, m, io):
    with ExitStack() as ctx:
        st = Store(nc, ctx)
        SLOTS = 3
        term = st.sb("term", [P, ST, COL])
        w_raw = st.sb("gw_raw", [P, SLOTS, COL])
        w_hi = st.sb("gw_hi", [P, SLOTS, COL], F32R)
        w_lo = st.sb("gw_lo", [P, SLOTS, COL], F32R)
        pt_hi = st.sb("pt_hi", [P, D_PLE // P, SEQ], F32R)
        pt_lo = st.sb("pt_lo", [P, D_PLE // P, SEQ], F32R)
        p_row = term[:, 0:4, :].rearrange("p a (b c) -> p (a b) c", b=2)
        bias = st.sb("pg_bias", [P, COL])
        best = st.sb("best", [P, ST, 8])
        bank = [st.ps(f"g_bank{s}", [P, COL]) for s in range(ST)]

        NP, NG = D_PLE // P, KT
        CH = NP + NG
        BLOCKS = D_MODEL // COL
        ROUNDS = TOPK // 8 // BLOCKS
        PICKED = ST - FIRST_PICKED
        p_in, bias_in = [sem(f"p_in{n}") for n in range(ST // 2)], sem("pg_bias_in")
        raw_in = [sem(f"gw_in{n}") for n in range(SLOTS)]
        hi_ok, lo_ok, chunk_used = sem("gw_hi_ok"), sem("gw_lo_ok"), sem("gw_used")
        p_turned, p_hi_ok, p_lo_ok = sem("p_turned"), sem("p_hi_ok"), sem("p_lo_ok")
        ple_done, ple_ok, gate_done, biased, sigmoid_ok, bank_free = (
            sem("ple_done"), sem("ple_ok"), sem("gate_done"), sem("g_biased"), sem("sigmoid_ok"), sem("g_bank_free"))
        term_out, pick_steps = [sem(f"term_out{n}") for n in range(ST // 2)], sem("pick_steps")
        masks_ok = sem("masks_ok")
        m.terms_stored = [(s, 16 * BLOCKS) for s in term_out]
        m.masks_done = masks_ok, 1
        m.gate_bank_free = lambda s: (bank_free, BLOCKS * ST + s + 1)
        out_cols = io["gate_term"].rearrange("(t p) n -> p t n", p=P)

        @block.sync
        def _(sp):
            sp.wait_ge(*m.index_weights_used)
            for n in range(len(p_in)):
                sp.dma_start(p_row[:, 2 * n:2 * n + 2, :], io["p"].rearrange("(n t p) d -> n p t d", p=P, t=2)[n]).then_inc(p_in[n], 16)

            sp.wait_ge(*m.index_dots_done)
            with sp.Fori(0, BLOCKS) as i:
                for c in range(CH):
                    sp.wait_ge(lo_ok, i * CH + c + 1)
                    rows = io["w_ple"][c * P:(c + 1) * P] if c < NP else io["w_pg"][(c - NP) * P:(c - NP + 1) * P]
                    sp.dma_start(w_raw[:, c % SLOTS, :], rows[:, bass.ds(i * COL, COL)]).then_inc(raw_in[c % SLOTS], 16)
                    if c == SLOTS:
                        sp.wait_ge(bank_free, (i + 1) * ST)
                        sp.dma_start(bias[:], io["b_pg"][bass.ds(i * COL, COL)].partition_broadcast(P)).then_inc(bias_in, 16)

        @block.gpsimd
        def _(pool):
            pool.sem_inc(lo_ok, SLOTS)
            with pool.Fori(0, BLOCKS) as i:
                for c in range(CH):
                    pool.wait_ge(hi_ok, i * CH + c + 1)
                    nc.gpsimd.tensor_tensor(w_lo[:, c % SLOTS, :], w_raw[:, c % SLOTS, :], f(w_hi[:, c % SLOTS, :]),
                                            ALU.subtract).then_inc(lo_ok, 1)

        @block.tensor
        def _(pe):
            for s in range(ST):
                if s == 0:
                    pe.wait_ge(*m.index_proj_read)
                if s == 2:
                    pe.wait_ge(*m.index_scored)
                pe.wait_ge(p_in[s // 2], 16)
                for k in range(NP):
                    last = nc.tensor.transpose(bank[s][:, bass.ts(k, P)], p_row[:, s, bass.ts(k, P)], m.ident)
                last.then_inc(p_turned, 1)
            pe.wait_ge(p_lo_ok, ST)
            with pe.Fori(0, BLOCKS) as i:
                for c in range(CH):
                    pe.wait_ge(lo_ok, i * CH + c + 1 + SLOTS)
                    for s in range(ST):
                        at = bass.ts(s, P)
                        if c == 0:
                            pe.wait_ge(bank_free, i * ST + s + 1)
                        if c == NP:
                            pe.wait_ge(ple_ok, i * ST + s + 1)
                        if c < NP:
                            last = matmul3(nc, bank[s][:], pt_hi[:, c, at], pt_lo[:, c, at], w_hi[:, c % SLOTS, :],
                                           w_lo[:, c % SLOTS, :], c == 0, c == NP - 1)
                        else:
                            k = c - NP
                            last = matmul3(nc, bank[s][:], m.x_hi[:, k, at], m.x_lo[:, k, at], w_hi[:, c % SLOTS, :],
                                           w_lo[:, c % SLOTS, :], k == 0, k == NG - 1)
                        if c == NP - 1:
                            last.then_inc(ple_done, 1)
                        elif c == CH - 1:
                            last.then_inc(gate_done, 1)
                        elif s == ST - 1:
                            last.then_inc(chunk_used, 1)

        counted = [c for c in range(CH) if c not in (NP - 1, CH - 1)]

        @block.scalar
        def _(act):
            def split_hi(i, c):
                c, i = c % CH, i + c // CH
                act.wait_ge(raw_in[c % SLOTS], 16 * (i * (CH // SLOTS) + c // SLOTS + 1))
                old = c - SLOTS
                if old % CH == NP - 1:
                    act.wait_ge(ple_done, (i + old // CH + 1) * ST)
                elif old % CH == CH - 1:
                    if not (isinstance(i, int) and i == 0):
                        act.wait_ge(gate_done, i * ST)
                elif old >= 0 or not (isinstance(i, int) and i == 0):
                    before = (i + old // CH) * len(counted) + counted.index(old % CH) + 1
                    act.wait_ge(chunk_used, before)
                nc.scalar.copy(w_hi[:, c % SLOTS, :], w_raw[:, c % SLOTS, :]).then_inc(hi_ok, 1)

            def column_block(i, last):
                for c in range(CH):
                    if c + 2 < CH or not last:
                        split_hi(i, c + 2)
                    if c == NP - 1:
                        for s in range(ST):
                            if s % 2 == 0 and not (isinstance(i, int) and i == 0):
                                act.wait_ge(term_out[s // 2], 16 * i)
                            act.wait_ge(ple_done, i * ST + s + 1)
                            nc.scalar.copy(term[:, s, :], bank[s][:]).then_inc(ple_ok, 1)
                for s in range(ST + 1):
                    if s < ST:
                        act.wait_ge(biased, i * ST + s + 1)
                        nc.scalar.activation(bank[s][:], bank[s][:], ACT.Sigmoid).then_inc(sigmoid_ok, 1)
                    if s and s % 2 == 0:
                        act.wait_ge(bank_free, i * ST + ST + s)
                        act.dma_start(out_cols[:, s - 2:s, bass.ds(i * COL, COL)], term[:, s - 2:s, :]).then_inc(term_out[s // 2 - 1], 16)

            act.wait_ge(*m.index_scored)
            for s in range(ST):
                act.wait_ge(p_turned, s + 1)
                nc.scalar.copy(pt_hi[:, :, bass.ts(s, P)], bank[s][:, 0:NP * P].rearrange("p (k q) -> p k q", k=NP)) \
                    .then_inc(p_hi_ok, 1)
            split_hi(0, 0)
            split_hi(0, 1)
            column_block(0, False)
            with act.Fori(1, BLOCKS - 1) as i:
                column_block(i, False)
            column_block(BLOCKS - 1, True)

        @block.vector
        def _(dve):
            dve.sem_inc(bank_free, ST)
            for s in range(ST):
                dve.wait_ge(p_hi_ok, s + 1)
                part = (slice(None), slice(None), bass.ts(s, P))
                nc.vector.tensor_tensor(pt_lo[part], bank[s][:, 0:NP * P].rearrange("p (k q) -> p k q", k=NP),
                                        f(pt_hi[part]), ALU.subtract).then_inc(p_lo_ok, 1)
            ch = Chain(dve, pick_steps)

            def rounds(first, n):
                group = [FIRST_PICKED + (first + j) % PICKED for j in range(n)]
                for b in group:
                    at = m.scores[:, SCORE_AT[b]:SCORE_AT[b] + (b + 1) * P]
                    ch.step(nc.vector.max(best[:, b, :], at))
                ch.wait()
                for b in group:
                    at = m.scores[:, SCORE_AT[b]:SCORE_AT[b] + (b + 1) * P]
                    ch.step(nc.vector.match_replace(out=at, in_to_replace=best[:, b, :], in_values=at, imm_value=TAKEN))
                ch.wait()

            EACH = PICKED * ROUNDS // KT

            def column_block(i, pick):
                pick()
                dve.wait_ge(bias_in, 16 * (i + 1))
                for s in range(ST + 1):
                    if s < ST:
                        dve.wait_ge(gate_done, i * ST + s + 1)
                        nc.vector.tensor_tensor(bank[s][:], bank[s][:], bias[:], ALU.add).then_inc(biased, 1)
                    if s:
                        dve.wait_ge(sigmoid_ok, i * ST + s)
                        nc.vector.tensor_tensor(term[:, s - 1, :], bank[s - 1][:], term[:, s - 1, :], ALU.mult) \
                            .then_inc(bank_free, 1)

            def picks():
                for c in range(KT):
                    rounds(c * EACH, EACH)

            def picks_and_masks():
                picks()
                for b in range(FIRST_PICKED, ST):
                    w = (b + 1) * P
                    ch.step(nc.vector.tensor_scalar(m.mask[:, MASK_AT[b]:MASK_AT[b] + w], m.scores[:, SCORE_AT[b]:SCORE_AT[b] + w],
                                                    0.5 * TAKEN, NEG, ALU.is_gt, ALU.mult))
                ch.link(nc.vector.memset(m.mask[:, 0:2 * P], 0.0))
                nc.vector.memset(m.mask[0:CHUNK, 2 * P - CHUNK:2 * P], NEG).then_inc(masks_ok, 1)
                dve.wait_ge(masks_ok, 1)

            with dve.Fori(0, BLOCKS - 1) as i:
                ch.enter(i, 2 * PICKED * ROUNDS)
                column_block(i, picks)
            ch.leave(BLOCKS - 1)
            column_block(BLOCKS - 1, picks_and_masks)


class Turn:

    def __init__(self, tiles, head, group, chunk0, raw0, round0, parts0, reads0):
        self.tiles = tiles
        self.head = head
        self.group = group
        self.chunk0 = chunk0
        self.raw0 = raw0
        self.round0 = round0
        self.parts0 = parts0
        self.reads0 = reads0


QK_AT = [2, 4, 6, 9, 13, 17, 21, 25]
EXP_AT = [3, 5, 7, 10, 14, 18, 22, 26]
NORM_AT = [3, 5, 7, 10, 15, 19, 23, 27]
TURN_AT = [4, 6, 9, 13, 17, 21, 25, 29]
PV_AT = [6, 8, 11, 15, 20, 24, 28, 31]
TABLE_AT = [14, 22]
GATE_AT = 4
ATTEND = 32


def block_rounds(b):
    return 1 + (b >= 4), b + max(0, b - 4)


HEAD_ROUNDS = sum(block_rounds(b)[0] for b in range(ST))
V_ROUNDS = 2


def heads_phase(nc, block, sem, m, io):
    with ExitStack() as ctx:
        st = Store(nc, ctx)
        SLOTS, LEAD, KC = 4, 3, 2
        PER = KT // KC
        w_raw = st.sb("hw_raw", [P, SLOTS, KC, P])
        w_hi = st.sb("hw_hi", [P, SLOTS, KC, P], F32R)
        w_lo = st.sb("hw_lo", [P, SLOTS, KC, P], F32R)
        pt = st.sb("h_pt", [P, ST, 2, P], F32R)
        gate = st.sb("gate", [P, SEQ])
        k_hi, k_lo = st.sb("k_hi", [P, SEQ], F32R), st.sb("k_lo", [P, SEQ], F32R)
        q_hi, q_lo = st.sb("q_hi", [P, SEQ], F32R), st.sb("q_lo", [P, SEQ], F32R)
        v_hi, v_lo = st.sb("v_hi", [P, SEQ], F32R), st.sb("v_lo", [P, SEQ], F32R)
        prob = st.sb("prob", [P, SEQ])
        tab = st.sb("h_tab", [P, 2, SEQ])
        tmp = st.sb("h_tmp", [P, 2 * COL])
        band, toeplitz = tmp[:, 0:BAND_TILES * P], tmp[:, BAND_TILES * P:(BAND_TILES + 2) * P]
        plain, swapped = tmp[:, 0:COL], tmp[:, COL:2 * COL]
        low = st.sb("low", [P, ST])
        total = st.sb("total", [P, ST])
        pv_low = st.sb("pv_low", [P, P])
        inv = st.sb("inv", [P, ST])
        proj = m.proj
        s_ps = st.ps("s_ps", [P, SEQ])
        t_ps = st.ps("t_ps", [P, COL])
        o_ps = st.ps("o_ps", [P, COL])
        t_tiles = t_ps[:].rearrange("p (t q) -> p t q", q=P)
        v_tiles = lambda v, r: v[:, bass.ts(r, COL)].rearrange("p (t d) -> p t d", d=P)

        raw_in = [sem(f"hw_in{n}") for n in range(SLOTS)]
        hi_ok, lo_ok, chunk_used = sem("hw_hi_ok"), sem("hw_lo_ok"), sem("hw_used")
        part_hi, part_lo, rope_read, roped, rope_steps = sem("h_part_hi"), sem("h_part_lo"), sem("h_rope_read"), sem("h_roped"), sem("h_rope_steps")
        v_read, gate_sig, gate_ok = sem("v_read"), sem("gate_sig"), sem("gate_ok")
        s_ok, low_ok, exp_ok, inv_ok, norm_ok = sem("s_ok"), sem("low_ok"), sem("exp_ok"), sem("inv_ok"), sem("norm_ok")
        turned, turned_hi, turned_lo, pv_ok, y_ok = sem("turned"), sem("turned_hi"), sem("turned_lo"), sem("pv_ok"), sem("y_ok")
        pv_steps = sem("pv_steps")
        y_out, toep_in, band_steps, band_ok = sem("y_out"), sem("toep_in"), sem("band_steps"), sem("band_ok")
        pos_in, tab_steps, rest_ok, tab_ok = sem("h_pos_in"), sem("h_tab_steps"), sem("h_rest_ok"), sem("h_tab_ok")
        SCALE = HEAD_DIM ** -0.5

        o_raw, o_hi, o_lo = (w[:].rearrange("p (a s) k n -> p a (s k n)", a=2) for w in (w_raw, w_hi, w_lo))
        y_stage_pair = st.sb("y_stage", [P, 2, COL])
        y_stage = [y_stage_pair[:, n, :] for n in range(2)]
        y_hi, y_lo = m.x_hi, m.x_lo
        o_in, y_in = [sem("po_in0"), sem("po_in1")], [sem("py_in0"), sem("py_in1")]
        o_hi_ok, o_lo_ok, o_used, y_hi_ok, y_lo_ok = sem("po_hi_ok"), sem("po_lo_ok"), sem("po_used"), sem("py_hi_ok"), sem("py_lo_ok")
        OUT_AT = [2 * k + 1 for k in range(KT)]
        OUT_SPLIT_AT = [max(0, 2 * k - 1) for k in range(KT)]
        LAST = H_A + H_B - 1

        A_TURN, B_TURN = 4 * PER, 2 * PER

        def turn_a(h, peeled=False):
            tiles = [("q", COL_QA + h, False), ("k", COL_KA + h, False), ("v", COL_VA + h, False), ("g", COL_GA + h, False)]
            if peeled:
                return Turn(tiles, None, "A", 0, 0, 0, 0, 0)
            return Turn(tiles, h - 1, "A", h * A_TURN, h * (A_TURN // SLOTS),
                        (h - 1) * (HEAD_ROUNDS + V_ROUNDS) + V_ROUNDS, h * 4, 0)

        def turn_mid():
            tiles = [("q", COL_QB, True), ("k", COL_KB, True), ("v", COL_VB, False), ("g", COL_GB, False)]
            return Turn(tiles, H_A - 1, "A", H_A * A_TURN, H_A * A_TURN // SLOTS,
                        (H_A - 1) * (HEAD_ROUNDS + V_ROUNDS) + V_ROUNDS, H_A * 4, 0)

        def turn_b(j, last=False):
            tiles = [] if last else [("q", COL_QB + 1 + j, True), ("g", COL_GB + 1 + j, False)]
            c0 = (H_A + 1) * A_TURN
            return Turn(tiles, H_A + j, "B", j * B_TURN + c0, j * (B_TURN // SLOTS) + c0 // SLOTS,
                        j * HEAD_ROUNDS + (H_A * (HEAD_ROUNDS + V_ROUNDS) + V_ROUNDS), j * 2 + (H_A + 1) * 4, j * 2 + 4)

        def all_turns(eng, run):
            run(turn_a(0, peeled=True), True)
            with eng.Fori(1, H_A) as h:
                run(turn_a(h), True)
            run(turn_mid(), True)
            with eng.Fori(0, H_B - 2) as j:
                run(turn_b(j), True)
            run(turn_b(H_B - 2), False)
            run(turn_b(H_B - 1, last=True), False)

        def wait(eng, s, value):
            if not (isinstance(value, int) and value <= 0):
                eng.wait_ge(s, value)

        def blocks_before(t, b):
            return t.head * ST + b

        def width(t, b):
            n = min(b + 1, BAND_TILES) if t.group == "A" else b + 1
            return n, b + 1 - n

        def score_at(w):
            return COL - w // 2 if w == COL + P else 0

        def positions(t):
            return range(max(KT * len(t.tiles), ATTEND if t.head is not None else 0))

        def role_at(t, role):
            return KT * (1 + [r for r, _, _ in t.tiles].index(role))

        def gate_at(t):
            return GATE_AT if t.tiles else 1

        def has(t, role):
            return any(r == role for r, _, _ in t.tiles)

        def ropes(t, role):
            return any(r == role and rot for r, _, rot in t.tiles)

        w_rows = io["w_in"].rearrange("(c k p) n -> c p k n", k=KC, p=P)

        m.last_scores = s_ok, (LAST + 1) * ST
        m.last_y = y_ok, (LAST + 1) * ST + 1
        m.y_staged_split = y_lo_ok, LAST
        m.y_all_split = y_lo_ok, KT + 1
        m.first_pass_done = o_used, KT

        @block.sync
        def _(sp):
            sp.wait_ge(*m.masks_done)

            def run(t, more):
                for c in range(PER * len(t.tiles)):
                    role, tile, _ = t.tiles[c // PER]
                    if t.head is None and c == 4:
                        for s, count in m.terms_stored:
                            sp.wait_ge(s, count)
                        sp.dma_start(gate[:].bitcast(I32), io["positions"].partition_broadcast(P)).then_inc(pos_in, 16)
                    wait(sp, lo_ok, t.chunk0 + (c - SLOTS + 1))
                    sp.dma_start(w_raw[:, c % SLOTS, :, :], w_rows[c % PER, :, :, bass.ds(tile * P, P)]) \
                        .then_inc(raw_in[c % SLOTS], 16)
                    if c == 4 and t.group == "A" and not ropes(t, "q"):
                        h = 0 if t.head is None else t.head + 1
                        wait(sp, band_ok, h)
                        sp.dma_start(toeplitz, io["rel_skew"][bass.ds(h, 1), :, :].rearrange("h p n -> p (h n)")) \
                            .then_inc(toep_in, 16)
            all_turns(sp, run)
            last = turn_b(H_B - 1, last=True)
            for k in range(KT):
                if k < 2:
                    sp.wait_ge(lo_ok, last.chunk0 - 2 * (1 - k))
                else:
                    sp.wait_ge(o_lo_ok, k - 1)
                sp.dma_start(o_raw[:, k % 2, :], io["w_out"][k * P:(k + 1) * P, 0:COL]).then_inc(o_in[k % 2], 16)
                if k < LAST:
                    if k >= 2:
                        sp.wait_ge(y_lo_ok, k - 1)
                    sp.wait_ge(y_out, 16 * (k + 2))
                    sp.dma_start(y_stage[k % 2], io["y"][k, :, 0:HALF]).then_inc(y_in[k % 2], 16)

        @block.gpsimd
        def _(pool):
            def run(t, more):
                for c in range(PER * len(t.tiles)):
                    if t.head is None and c < LEAD:
                        pool.wait_ge(raw_in[c], 16)
                        nc.gpsimd.tensor_copy(w_hi[:, c, :, :], w_raw[:, c, :, :]).then_inc(hi_ok, 1)
                    pool.wait_ge(hi_ok, t.chunk0 + (c + 1))
                    nc.gpsimd.tensor_tensor(w_lo[:, c % SLOTS, :, :], w_raw[:, c % SLOTS, :, :],
                                            f(w_hi[:, c % SLOTS, :, :]), ALU.subtract).then_inc(lo_ok, 1)
                    if c == 2 * PER and t.group == "A" and not ropes(t, "q"):
                        h = 0 if t.head is None else t.head + 1
                        if t.head is not None:
                            pool.wait_ge(low_ok, blocks_before(t, ST))
                        hold(pool, toep_in, (h + 1) * 16)
                        near = (BAND_TILES - 2) * P
                        nc.gpsimd.tensor_scalar(band[:, near:], toeplitz, 1 / SCALE, None, ALU.mult).then_inc(band_steps, 1)
                        nc.gpsimd.tensor_scalar(band[:, 0:near], toeplitz[:, 0:1].to_broadcast([P, near]), 1 / SCALE, None,
                                                ALU.mult).then_inc(band_steps, 1)
                        hold(pool, band_steps, h * 3 + 2)
                        nc.gpsimd.memset(band[CHUNK:P, 0:CHUNK], NEG).then_inc(band_steps, 1)
                        hold(pool, band_steps, h * 3 + 3)
                        nc.gpsimd.memset(band[0:CHUNK, BAND_TILES * P - CHUNK:], NEG).then_inc(band_ok, 1)
            all_turns(pool, run)
            for k in range(KT):
                pool.wait_ge(o_hi_ok, k + 1)
                nc.gpsimd.tensor_tensor(o_lo[:, k % 2, :], o_raw[:, k % 2, :], f(o_hi[:, k % 2, :]), ALU.subtract).then_inc(o_lo_ok, 1)

        @block.tensor
        def _(pe):
            def scores(t, b):
                n, first = width(t, b)
                pe.wait_ge(exp_ok, blocks_before(t, b) + 1)
                if b == 0:
                    pe.wait_ge(part_lo, t.parts0 if t.group == "A" else t.parts0 - 1)
                if b == ST // 2 and t.group == "B":
                    pe.wait_ge(part_lo, t.parts0)
                start = score_at(n * P)
                cuts = [start] + [c for c in (COL,) if c < start + n * P] + [start + n * P]
                for c0, c1 in zip(cuts, cuts[1:]):
                    at = slice(first * P + c0 - start, first * P + c1 - start)
                    last = matmul3(nc, s_ps[:, c0:c1], q_hi[:, bass.ts(b, P)], q_lo[:, bass.ts(b, P)], k_hi[:, at], k_lo[:, at],
                                   True, True)
                last.then_inc(s_ok, 1)

            def turn_round(t, rnd, src_tiles):
                wait(pe, turned_lo, rnd)
                for j, i in enumerate(src_tiles):
                    last = nc.tensor.transpose(t_ps[:, bass.ts(j, P)], prob[:, bass.ts(i, P)], m.ident)
                last.then_inc(turned, 1)

            def pv(t, b):
                n, first = width(t, b)
                rounds, before = block_rounds(b)
                pe.wait_ge(turned_lo, t.round0 + (before + rounds))
                pe.wait_ge(y_ok, blocks_before(t, b) + 1)
                for i in range(n):
                    v_at = bass.ts(first + i, P)
                    nc.tensor.matmul(o_ps[:, 0:2 * P], v_hi[:, v_at], pt[:, i, :, :], start=i == 0, stop=False)
                    last = nc.tensor.matmul(o_ps[:, 0:P], v_lo[:, v_at], pt[:, i, 0, :], start=False, stop=i == n - 1)
                last.then_inc(pv_ok, 1)

            def out_product(t, k):
                pe.wait_ge(o_lo_ok, k + 1)
                pe.wait_ge(y_lo_ok, k + 1)
                for s in range(HALF // P):
                    if k == 0 and s == 0:
                        pe.wait_ge(rope_read, t.reads0)
                    if k == 0 and s == 2:
                        pe.wait_ge(gate_ok, t.head + 1)
                    last = matmul3(nc, proj[s // 2][:, bass.ts(s % 2, COL)], y_hi[:, k, bass.ts(s, P)], y_lo[:, k, bass.ts(s, P)],
                                   o_hi[:, k % 2, :], o_lo[:, k % 2, :], k == 0, k == KT - 1)
                last.then_inc(o_used, 1)

            def run(t, more):
                for pos in positions(t):
                    if t.head is not None and pos < ATTEND:
                        if pos in PV_AT:
                            pv(t, PV_AT.index(pos))
                        for r in range(2):
                            if pos - r in TURN_AT:
                                b = TURN_AT.index(pos - r)
                                rounds, before = block_rounds(b)
                                if r < rounds:
                                    if r == 0:
                                        pe.wait_ge(norm_ok, blocks_before(t, b + 1))
                                    turn_round(t, t.round0 + (before + r), range(4 * r, min(4 * r + 4, width(t, b)[0])))
                        if pos in QK_AT:
                            scores(t, QK_AT.index(pos))
                    if has(t, "v"):
                        for r in range(V_ROUNDS):
                            if pos == role_at(t, "v") + 3 + 2 * r:
                                if r == 0:
                                    pe.wait_ge(v_read, 1 if t.head is None else t.head + 2)
                                turn_round(t, t.round0 + ((0 if t.head is None else HEAD_ROUNDS) + r), range(4 * r, 4 * r + 4))
                    if not t.tiles and pos in OUT_AT:
                        out_product(t, OUT_AT.index(pos))
                    if pos >= KT * len(t.tiles):
                        continue
                    tile, k = pos // KT, pos % KT
                    if k == 0 and t.head is not None:
                        if tile == 0:
                            pe.wait_ge(v_read, t.head + 1 if t.group == "A" else H_A + 1)
                            if t.group == "B":
                                pe.wait_ge(rope_read, t.reads0)
                        elif tile == 1:
                            pe.wait_ge(gate_ok, t.head + 1)
                    if k == 0 and t.head is None and tile < 2:
                        pe.wait_ge(*m.gate_bank_free(1 if tile == 0 else ST - 1))
                    if k == 0 and tile >= 2:
                        if ropes(t, "q"):
                            pe.wait_ge(rope_read, t.reads0 + 2 * (tile - 1))
                        else:
                            pe.wait_ge(part_lo, t.parts0 + 2 * (tile - 1))
                    c = pos // KC
                    if pos % KC == 0:
                        pe.wait_ge(lo_ok, t.chunk0 + (c + 1))
                    for h in range(2):
                        at = slice(h * COL, (h + 1) * COL)
                        last = matmul3(nc, proj[tile % 2][:, at], w_hi[:, c % SLOTS, pos % KC, :], w_lo[:, c % SLOTS, pos % KC, :],
                                       m.x_hi[:, k, at], m.x_lo[:, k, at], k == 0, k == KT - 1)
                    if pos % KC == KC - 1:
                        last.then_inc(chunk_used, 1)
            pe.sem_inc(pv_ok, 1)
            all_turns(pe, run)

        def part(role, h):
            at = slice(h * COL, (h + 1) * COL)
            return (q_hi[:, at], q_lo[:, at]) if role == "q" else (k_hi[:, at], k_lo[:, at])

        ROPE = {"q": [(26, 27, 28), (30, 30, 31)], "k": [(33, 34, 35), (36, 37, 38)]}
        PLAIN = {"q": [(27, 28), (27, 28)], "k": [(33, 34), (33, 34)]}

        @block.scalar
        def _(act):
            def split_hi(t, c):
                act.wait_ge(raw_in[c % SLOTS], (t.raw0 + (c // SLOTS + 1)) * 16)
                wait(act, chunk_used, t.chunk0 + (c - SLOTS + 1))
                nc.scalar.copy(w_hi[:, c % SLOTS, :, :], w_raw[:, c % SLOTS, :, :]).then_inc(hi_ok, 1)

            def turned_part(t, rnd, dst_hi, n):
                act.wait_ge(turned, rnd + 1)
                nc.scalar.copy(dst_hi, t_tiles[:, 0:n, :]).then_inc(turned_hi, 1)

            def out_parts(t, k):
                act.wait_ge(o_in[k % 2], 16 * (k // 2 + 1))
                if k < 2:
                    act.wait_ge(chunk_used, t.chunk0)
                else:
                    act.wait_ge(o_used, k - 1)
                nc.scalar.copy(o_hi[:, k % 2, :], o_raw[:, k % 2, :]).then_inc(o_hi_ok, 1)
                if k < LAST:
                    act.wait_ge(y_in[k % 2], 16 * (k // 2 + 1))
                    nc.scalar.copy(y_hi[:, k, 0:HALF], y_stage[k % 2]).then_inc(y_hi_ok, 1)
                else:
                    act.wait_ge(y_ok, blocks_before(t, HALF // P) + 1)
                    nc.scalar.copy(y_hi[:, k, 0:HALF], gate[:, 0:HALF]).then_inc(y_hi_ok, 1)

            def run(t, more):
                for pos in positions(t):
                    if not t.tiles:
                        for k in range(KT):
                            if OUT_SPLIT_AT[k] == pos:
                                out_parts(t, k)
                    if pos == gate_at(t) and t.head is not None:
                        act.wait_ge(y_out, (t.head + 1) * 16)
                        hold(act, chunk_used, t.chunk0)
                        col = COL_GA + t.head if t.group == "A" else t.head + (COL_GB - H_A)
                        nc.scalar.activation(gate[:], proj[1][:], ACT.Sigmoid, bias=m.b_col[:, bass.ds(col, 1)]).then_inc(gate_sig, 1)
                    if t.head is None and pos in TABLE_AT:
                        n = TABLE_AT.index(pos)
                        act.wait_ge(rest_ok, n + 1)
                        nc.scalar.activation(tab[:, n, :], tab[:, n, :], ACT.Sin).then_inc(tab_ok, 1)
                    if t.head is not None and pos < ATTEND:
                        for r in range(2):
                            if pos - r in TURN_AT:
                                b = TURN_AT.index(pos - r)
                                rounds, before = block_rounds(b)
                                if r < rounds:
                                    if r == 0:
                                        act.wait_ge(pv_ok, blocks_before(t, b) + 1)
                                    n = min(4, width(t, b)[0] - 4 * r)
                                    turned_part(t, t.round0 + (before + r), pt[:, 4 * r:4 * r + n, 0, :], n)
                        if pos in EXP_AT:
                            b = EXP_AT.index(pos)
                            w = width(t, b)[0] * P
                            act.wait_ge(low_ok, blocks_before(t, b + 1))
                            wait(act, turned, t.round0 + block_rounds(b)[1])
                            c0 = score_at(w)
                            nc.scalar.activation(prob[:, 0:w], s_ps[:, c0:c0 + w], ACT.Exp, bias=low[:, b:b + 1], scale=-1.0,
                                                 accum_out=total[:, b:b + 1]).then_inc(exp_ok, 1)
                    for role in "qk":
                        if not has(t, role):
                            continue
                        col = [c for r, c, _ in t.tiles if r == role][0]
                        bias = m.b_col[:, bass.ds(col, 1)]
                        done = role_at(t, role)
                        for h in range(2):
                            at = slice(h * COL, (h + 1) * COL)
                            number = 2 * (role == "k") + h
                            if ropes(t, role):
                                read, _, split = ROPE[role][h]
                                if pos == read:
                                    act.wait_ge(part_lo, t.parts0 + number)
                                    hold(act, chunk_used, t.chunk0 + done // KC)
                                    nc.scalar.activation(plain, proj[done // KT - 1][:, at], ACT.Identity, bias=bias)
                                    for lo, hi in ((0, 64), (64, 0)):
                                        last = nc.scalar.activation(swapped[lo:lo + 64, :], proj[done // KT - 1][hi:hi + 64, at],
                                                                    ACT.Identity, bias=bias[hi:hi + 64, :])
                                    last.then_inc(rope_read, 1)
                                if pos == split:
                                    act.wait_ge(roped, t.reads0 + (number + 1))
                                    wait(act, s_ok, blocks_before(t, ST))
                                    nc.scalar.copy(part(role, h)[0], plain).then_inc(part_hi, 1)
                            elif pos == PLAIN[role][h][0]:
                                if t.head is not None:
                                    act.wait_ge(s_ok, blocks_before(t, ST))
                                hold(act, chunk_used, t.chunk0 + done // KC)
                                nc.scalar.activation(part(role, h)[0], proj[done // KT - 1][:, at], ACT.Identity, bias=bias) \
                                    .then_inc(part_hi, 1)
                    if has(t, "v"):
                        done = role_at(t, "v")
                        r0 = t.round0 + (0 if t.head is None else HEAD_ROUNDS)
                        if pos == done + 1:
                            wait(act, turned, r0)
                            hold(act, chunk_used, t.chunk0 + done // KC)
                            nc.scalar.activation(prob[:], proj[0][:], ACT.Identity, bias=m.b_col[:, bass.ds(t.tiles[2][1], 1)]) \
                                .then_inc(v_read, 1)
                        for r in range(V_ROUNDS):
                            if pos == done + 3 + 2 * r:
                                if r == 0 and t.head is not None:
                                    act.wait_ge(pv_ok, blocks_before(t, ST) + 1)
                                turned_part(t, r0 + r, v_tiles(v_hi, r), 4)
                    if pos % KC == 1 and pos < KT * len(t.tiles):
                        c = pos // KC + LEAD
                        if c < PER * len(t.tiles) or more:
                            split_hi(t, c)
                if t.head is not None:
                    act.wait_ge(y_ok, blocks_before(t, ST) + 1)
                if not t.tiles:
                    nc.scalar.copy(y_hi[:, LAST, HALF:], gate[:, HALF:]).then_inc(y_hi_ok, 1)
                elif t.head is not None:
                    act.dma_start(io["y"][bass.ds(t.head, 1), :, :].rearrange("h p s -> p (h s)"), gate[:]).then_inc(y_out, 16)
            act.sem_inc(exp_ok, 1)
            act.sem_inc(y_out, 16)
            act.wait_ge(lo_ok, LEAD)
            all_turns(act, run)
            act.wait_ge(y_out, (LAST + 1) * 16)

        @block.vector
        def _(dve):
            def turned_part(rnd, dst_hi, dst_lo, n):
                dve.wait_ge(turned_hi, rnd + 1)
                nc.vector.tensor_tensor(dst_lo, t_tiles[:, 0:n, :], f(dst_hi), ALU.subtract).then_inc(turned_lo, 1)

            def run(t, more):
                for pos in positions(t):
                    if not t.tiles:
                        for k in range(KT):
                            if OUT_SPLIT_AT[k] == pos:
                                src = y_stage[k % 2] if k < LAST else gate[:, 0:HALF]
                                dve.wait_ge(y_hi_ok, k + 1)
                                nc.vector.tensor_tensor(y_lo[:, k, 0:HALF], src, f(y_hi[:, k, 0:HALF]), ALU.subtract).then_inc(y_lo_ok, 1)
                    if pos == gate_at(t) + (1 if t.tiles else 0) and t.head is not None:
                        dve.wait_ge(gate_sig, t.head + 1)
                        col = COL_GA + t.head if t.group == "A" else t.head + (COL_GB - H_A)
                        nc.vector.scalar_tensor_tensor(gate[:], proj[1][:], m.b_col[:, bass.ds(col, 1)], gate[:], ALU.add, ALU.mult) \
                            .then_inc(gate_ok, 1)
                    if t.head is not None and pos < ATTEND:
                        if pos in PV_AT:
                            b = PV_AT.index(pos)
                            dve.wait_ge(pv_ok, blocks_before(t, b + 1) + 1)
                            dve.wait_ge(gate_ok, t.head + 1)
                            nc.vector.tensor_copy(pv_low[:], o_ps[:, P:2 * P]).then_inc(pv_steps, 1)
                            dve.wait_ge(pv_steps, blocks_before(t, b) * 2 + 1)
                            nc.vector.tensor_tensor(pv_low[:], o_ps[:, 0:P], pv_low[:], ALU.add).then_inc(pv_steps, 1)
                            dve.wait_ge(pv_steps, blocks_before(t, b) * 2 + 2)
                            nc.vector.tensor_tensor(gate[:, bass.ts(b, P)], pv_low[:], gate[:, bass.ts(b, P)], ALU.mult) \
                                .then_inc(y_ok, 1)
                        for r in range(2):
                            if pos - r in TURN_AT:
                                b = TURN_AT.index(pos - r)
                                rounds, before = block_rounds(b)
                                if r < rounds:
                                    n = min(4, width(t, b)[0] - 4 * r)
                                    turned_part(t.round0 + (before + r), pt[:, 4 * r:4 * r + n, 0, :], pt[:, 4 * r:4 * r + n, 1, :], n)
                        if pos in QK_AT:
                            b = QK_AT.index(pos)
                            w = width(t, b)[0] * P
                            if t.group == "A":
                                bias = band[:, BAND_TILES * P - w:]
                                if b == 0:
                                    dve.wait_ge(band_ok, t.head + 1)
                            else:
                                bias = m.mask[:, MASK_AT[b]:MASK_AT[b] + w]
                            hold(dve, s_ok, blocks_before(t, b + 1))
                            scored = s_ps[:, score_at(w):score_at(w) + w]
                            nc.vector.tensor_tensor_reduce(out=scored, in0=scored, in1=bias, scale=-SCALE, scalar=3e38,
                                                           op0=ALU.add, op1=ALU.min, accum_out=low[:, b:b + 1]).then_inc(low_ok, 1)
                        if pos in NORM_AT:
                            b = NORM_AT.index(pos)
                            w = width(t, b)[0] * P
                            dve.wait_ge(exp_ok, blocks_before(t, b + 1) + 1)
                            nc.vector.reciprocal(inv[:, b:b + 1], total[:, b:b + 1]).then_inc(inv_ok, 1)
                            dve.wait_ge(inv_ok, blocks_before(t, b + 1))
                            nc.vector.tensor_scalar(prob[:, 0:w], prob[:, 0:w], inv[:, b:b + 1], None, ALU.mult).then_inc(norm_ok, 1)
                    for role in "qk":
                        if not has(t, role):
                            continue
                        col = [c for r, c, _ in t.tiles if r == role][0]
                        done = role_at(t, role)
                        for h in range(2):
                            at = slice(h * COL, (h + 1) * COL)
                            number = 2 * (role == "k") + h
                            hi, lo = part(role, h)
                            if ropes(t, role):
                                _, rotate, split = ROPE[role][h]
                                if pos == rotate:
                                    dve.wait_ge(tab_ok, 2)
                                    dve.wait_ge(rope_read, t.reads0 + (number + 1))
                                    nc.vector.tensor_tensor(plain, plain, tab[:, 1, at], ALU.mult).then_inc(rope_steps, 1)
                                    nc.vector.tensor_tensor(swapped, swapped, tab[:, 0, at], ALU.mult).then_inc(rope_steps, 1)
                                    dve.wait_ge(rope_steps, t.reads0 * 2 + (2 * number + 2))
                                    nc.vector.tensor_tensor(plain, plain, swapped, ALU.add).then_inc(roped, 1)
                                if pos == split:
                                    dve.wait_ge(part_hi, t.parts0 + (number + 1))
                                    nc.vector.tensor_tensor(lo, plain, f(hi), ALU.subtract).then_inc(part_lo, 1)
                            elif pos == PLAIN[role][h][1]:
                                dve.wait_ge(part_hi, t.parts0 + (number + 1))
                                nc.vector.scalar_tensor_tensor(lo, proj[done // KT - 1][:, at], m.b_col[:, bass.ds(col, 1)], f(hi),
                                                               ALU.add, ALU.subtract).then_inc(part_lo, 1)
                    if has(t, "v"):
                        r0 = t.round0 + (0 if t.head is None else HEAD_ROUNDS)
                        for r in range(V_ROUNDS):
                            if pos == role_at(t, "v") + 3 + 2 * r:
                                turned_part(r0 + r, v_tiles(v_hi, r), v_tiles(v_lo, r), 4)
            dve.sem_inc(y_ok, 1)
            tc = Chain(dve, tab_steps)
            dve.wait_ge(pos_in, 16)
            tc.link(nc.vector.tensor_copy(prob[:], gate[:].bitcast(I32)))
            tc.link(nc.vector.tensor_scalar(prob[:], prob[:], m.rotary[:, 1:2], None, ALU.mult))
            for n, quarter in enumerate((0.0, 0.25)):
                rotary_argument(nc, tc.link, prob[:], gate[:], tab[:, n, :], quarter, m.rotary[:, 3:4]).then_inc(rest_ok, 1)
            all_turns(dve, run)
            dve.wait_ge(y_hi_ok, KT + 1)
            nc.vector.tensor_tensor(y_lo[:, LAST, HALF:], gate[:, HALF:], f(y_hi[:, LAST, HALF:]), ALU.subtract).then_inc(y_lo_ok, 1)
            dve.wait_ge(y_lo_ok, KT + 1)


class Mem:
    pass


PASSES = 2 * D_MODEL // COL
HELD = KT // 2
SPACING = 3


def pass_pair(first):
    plain = [(first, k) for k in range(KT)] + [(first + 1, k) for k in range(KT - HELD)]
    order = []
    for n, chunk in enumerate(plain):
        order.append(chunk)
        if n % SPACING == SPACING - 1:
            order.append((first + 1, KT - HELD + n // SPACING))
    return order


def out_phase(nc, block, sem, m, io):
    with ExitStack() as ctx:
        st = Store(nc, ctx)
        RAW, SLOTS, STAGES = 4, 4, 3
        NS, NQ = HALF // P, D_MODEL // COL
        row = st.sb("row", [P, NS, D_MODEL])
        stage = st.sb("stage", [P, STAGES, COL])
        w_raw = st.sb("ow_raw", [P, RAW, COL])
        ln_g, ln_b = st.sb("ln_g", [P, D_MODEL]), st.sb("ln_b", [P, D_MODEL])
        w_hi = st.sb("ow_hi", [P, SLOTS, COL], F32R)
        w_lo = st.sb("ow_lo", [P, SLOTS, COL], F32R)
        stats = st.sb("stats", [P, NS, NQ, 6])
        mean_var = st.sb("mean_var", [P, NS, 2])
        dev = st.sb("dev", [P, NS, 4])
        odd_bank = [st.ps(f"o_bank{n}", [P, COL])[:] for n in range(NS)]
        even_bank = [m.proj[s // 2][:, bass.ts(s % 2, COL)] for s in range(NS)]
        y_hi, y_lo = m.x_hi, m.x_lo

        raw_in = [sem(f"ow_in{n}") for n in range(RAW)]
        stage_in = [sem(f"stage_in{n}") for n in range(STAGES)]
        hi_ok, lo_ok, chunk_used, out_done, bank_free = (
            sem("ow_hi_ok"), sem("ow_lo_ok"), sem("ow_used"), sem("out_done"), sem("o_bank_free"))
        y_hi_ok, stage_used = sem("y_hi_ok"), sem("stage_used")
        term_in = [sem(f"term_in{s}") for s in range(NS)]
        row_out = [sem(f"row_out{s}") for s in range(NS)]
        ln_in, ln_steps, root_in, root_ok, ln_ok = sem("ln_in"), sem("ln_steps"), sem("root_in"), sem("root_ok"), sem("ln_ok")
        scale_ok, unit_ok, scaled, last_ok = sem("scale_ok"), sem("unit_ok"), sem("scaled"), sem("last_ok")

        held = lambda c: c[0] >= NQ and c[0] % 2 == 1 and c[1] >= KT - HELD
        first_half = [(q, k) for q in range(1, NQ) for k in range(KT)]
        order = first_half + pass_pair(NQ) + pass_pair(NQ + 2)
        plain = [c for c in order if not held(c)]
        counted = [c for c in plain if c[1] < KT - 1]
        FIRST_ROW_K = RAW - 1
        PAIR = 2 * KT

        x_item = lambda half, j: j if half == 0 else 2 * KT - 1 + j
        y_item = lambda k: KT + k
        w_rows = io["w_out"].rearrange("(k p) n -> k p n", p=P)
        rows_of = lambda t, half, s: t.rearrange("(h s p) n -> h s p n", h=2, p=P)[half, s]

        def x_beside(q, k):
            late = k - FIRST_ROW_K
            if q == 1 and late < 0:
                return []
            if q == 1 and late < FIRST_ROW_K:
                return [2 * late, 2 * late + 1]
            return [k] if q in (1, NQ + 2) else []

        def parts(c):
            if held(c):
                return y_hi[:, c[1] - (KT - HELD), 0:HALF], y_lo[:, c[1] - (KT - HELD), 0:HALF]
            return w_hi[:, c[1] % SLOTS, :], w_lo[:, c[1] % SLOTS, :]

        @block.sync
        def _(sp):
            def item(n, src):
                if n >= STAGES:
                    sp.wait_ge(stage_used, n - STAGES + 1)
                sp.dma_start(stage[:, n % STAGES, :], src).then_inc(stage_in[n % STAGES], 16)

            sp.wait_ge(*m.last_scores)
            for n, (q, k) in enumerate(order):
                if n >= RAW:
                    sp.wait_ge(lo_ok, n - RAW + 1)
                sp.dma_start(w_raw[:, n % RAW, :], w_rows[k, :, bass.ts(q % NQ, COL)]).then_inc(raw_in[n % RAW], 16)
                if held((q, k)):
                    continue
                if (q, k) == (1, FIRST_ROW_K):
                    sp.wait_ge(*m.first_pass_done)
                    sp.wait_ge(*m.y_all_split)
                if q == 1 and FIRST_ROW_K <= k < FIRST_ROW_K + NS:
                    s = k - FIRST_ROW_K
                    sp.dma_start(row[:, s, :], rows_of(io["gate_term"], 0, s)).then_inc(term_in[s], 16)
                for j in x_beside(q, k):
                    half = q // NQ
                    item(x_item(half, j), rows_of(io["x"], half, j // NQ)[:, bass.ts(j % NQ, COL)])
                if q == 2 and k < KT - 1:
                    item(y_item(k), io["y"][k, :, HALF:])
                if q == 3 and k == 0:
                    sp.dma_start(ln_g[:], io["ln_g"].partition_broadcast(P)).then_inc(ln_in, 16)
                    sp.dma_start(ln_b[:], io["ln_b"].partition_broadcast(P)).then_inc(ln_in, 16)
                for s in range(NS):
                    if q == NQ and k == 5 + 2 * s:
                        sp.wait_ge(ln_ok, s + 1)
                        sp.dma_start(rows_of(io["out"], 0, s), row[:, s, :]).then_inc(row_out[s], 16)
                    if q == NQ + 1 and k == 2 * s:
                        sp.wait_ge(row_out[s], 16)
                        sp.dma_start(row[:, s, :], rows_of(io["gate_term"], 1, s)).then_inc(term_in[s], 16)
            for s in range(NS):
                for h in range(2):
                    if s == NS - 1:
                        sp.wait_ge(last_ok, h + 1)
                    else:
                        sp.wait_ge(ln_ok, NS + 2 * s + h + 1)
                    at = bass.ts(h, D_MODEL // 2)
                    sp.dma_start(rows_of(io["out"], 1, s)[:, at], row[:, s, at]).then_inc(row_out[s], 16)
            for s in range(NS):
                sp.wait_ge(row_out[s], 48)

        @block.gpsimd
        def _(pool):
            def split_lo(n, c, raw):
                pool.wait_ge(hi_ok, n)
                hi, lo = parts(c)
                nc.gpsimd.tensor_tensor(lo, w_raw[:, raw, :], f(hi), ALU.subtract).then_inc(lo_ok, 1)

            pool.wait_ge(*m.y_staged_split)
            with pool.Fori(0, len(first_half) // SLOTS) as i:
                for c in range(SLOTS):
                    split_lo(i * SLOTS + (c + 1), first_half[c], c % RAW)
            with pool.Fori(0, 2) as i:
                for n, c in enumerate(pass_pair(NQ)):
                    split_lo(i * PAIR + (len(first_half) + n + 1), c, n % RAW)
            for s in range(NS - 1):
                for h in range(2):
                    at = bass.ts(h, D_MODEL // 2)
                    pool.wait_ge(scaled, 2 * s + h + 1)
                    nc.gpsimd.tensor_tensor(row[:, s, at], row[:, s, at], ln_b[:, at], ALU.add).then_inc(ln_ok, 1)

        @block.tensor
        def _(pe):
            def product(bank, c, s, release):
                half, k = c[0] // NQ, c[1]
                at = bass.ts(half * NS + s, P)
                hi, lo = parts(c)
                last = matmul3(nc, bank[s], y_hi[:, k, at], y_lo[:, k, at], hi, lo, k == 0, k == KT - 1)
                if k == KT - 1:
                    last.then_inc(out_done, 1)
                elif release:
                    last.then_inc(chunk_used, 1)

            def one_pass(q, chunks_before, free_before, in_order):
                bank = even_bank if q % 2 == 0 else odd_bank
                for k in range(KT):
                    c = (q, k)
                    if held(c):
                        continue
                    pe.wait_ge(lo_ok, chunks_before + (in_order.index(c) + 1))
                    for s in range(NS):
                        if k == 0 and free_before is not None:
                            pe.wait_ge(bank_free, free_before + (s + 1))
                        if q == 1 and k == 0 and s == NS - 1:
                            pe.wait_ge(*m.last_y)
                        product(bank, c, s, s == NS - 1)
                if held((q, KT - 1)):
                    for s in range(NS):
                        for k in range(KT - HELD, KT):
                            if s == 0:
                                pe.wait_ge(lo_ok, chunks_before + (in_order.index((q, k)) + 1))
                            product(bank, (q, k), s, False)

            one_pass(1, 0, None, first_half)
            one_pass(2, 0, 0, first_half)
            one_pass(3, 0, NS, first_half)
            pe.wait_ge(stage_used, y_item(KT - 2) + 1)
            with pe.Fori(0, 2) as i:
                one_pass(NQ, i * PAIR + len(first_half), i * 2 * NS + 2 * NS, pass_pair(NQ))
                one_pass(NQ + 1, i * PAIR + len(first_half), i * 2 * NS + 3 * NS, pass_pair(NQ))

        @block.scalar
        def _(act):
            def split_hi(n, c):
                act.wait_ge(raw_in[n % RAW], 16 * (n // RAW + 1))
                q, k = c
                if held(c):
                    act.wait_ge(out_done, (q - 2) * NS)
                elif plain.index(c) >= SLOTS:
                    old = plain[plain.index(c) - SLOTS]
                    if old in counted:
                        act.wait_ge(chunk_used, counted.index(old) + 1)
                    else:
                        act.wait_ge(out_done, old[0] * NS)
                nc.scalar.copy(parts(c)[0], w_raw[:, n % RAW, :]).then_inc(hi_ok, 1)

            def root(half, s):
                act.wait_ge(root_in, half * NS + s + 1)
                nc.scalar.activation(dev[:, s, 1:2], dev[:, s, 0:1], ACT.Sqrt).then_inc(root_ok, 1)

            for n, (q, k) in enumerate(order):
                if q == 2 and k < KT - 1:
                    item = y_item(k)
                    act.wait_ge(stage_in[item % STAGES], 16 * (item // STAGES + 1))
                    nc.scalar.copy(y_hi[:, k, HALF:], stage[:, item % STAGES, :]).then_inc(y_hi_ok, 1)
                split_hi(n, (q, k))
                if q == NQ and k in (2, 4, 6, 8):
                    root(0, (2, 4, 6, 8).index(k))
            for s in range(NS):
                root(1, s)
                act.wait_ge(scale_ok, s + 1)
                for h in range(2):
                    at = bass.ts(h, D_MODEL // 2)
                    nc.scalar.activation(row[:, s, at], row[:, s, at], ACT.Identity, bias=dev[:, s, 3:4], scale=dev[:, s, 2:3]) \
                        .then_inc(unit_ok, 1)

        @block.vector
        def _(dve):
            ch = Chain(dve, ln_steps)

            def add_x(half, j):
                n = x_item(half, j)
                at = row[:, j // NQ, bass.ts(j % NQ, COL)]
                dve.wait_ge(stage_in[n % STAGES], 16 * (n // STAGES + 1))
                nc.vector.scalar_tensor_tensor(at, stage[:, n % STAGES, :], ALPHA, at, ALU.mult, ALU.add).then_inc(stage_used, 1)

            def split_y(k):
                n = y_item(k)
                dve.wait_ge(y_hi_ok, k + 1)
                nc.vector.tensor_tensor(y_lo[:, k, HALF:], stage[:, n % STAGES, :], f(y_hi[:, k, HALF:]), ALU.subtract) \
                    .then_inc(stage_used, 1)

            def add_y(q, s):
                at = row[:, s, bass.ts(q % NQ, COL)]
                if q:
                    dve.wait_ge(out_done, (q - 1) * NS + s + 1)
                dve.wait_ge(term_in[s], 16 * (q // NQ + 1))
                bank = even_bank if q % 2 == 0 else odd_bank
                nc.vector.tensor_tensor(at, bank[s], at, ALU.add).then_inc(bank_free, 1)

            def add_pass(q):
                for s in range(NS):
                    add_y(q, s)
                dve.wait_ge(bank_free, (q + 1) * NS)

            def row_stats(s, cols):
                for c in cols:
                    ch.step(nc.vector.bn_stats(stats[:, s, c, :], row[:, s, bass.ts(c, COL)]))

            def deviation(s):
                ch.wait()
                ch.link(nc.vector.bn_aggr(mean_var[:, s, :], stats[:, s, :, :]))
                nc.vector.tensor_scalar(dev[:, s, 0:1], mean_var[:, s, 1:2], LN_EPS, None, ALU.add).then_inc(root_in, 1)

            def one_over_root(half, s):
                dve.wait_ge(root_ok, half * NS + s + 1)
                ch.link(nc.vector.reciprocal(dev[:, s, 2:3], dev[:, s, 1:2]))

            def normalise(s):
                one_over_root(0, s)
                halves = [bass.ts(h, D_MODEL // 2) for h in range(2)]
                for at in halves:
                    ch.step(nc.vector.scalar_tensor_tensor(row[:, s, at], row[:, s, at], mean_var[:, s, 0:1], ln_g[:, at],
                                                           ALU.subtract, ALU.mult))
                ch.wait()
                nc.vector.scalar_tensor_tensor(row[:, s, :], row[:, s, :], dev[:, s, 2:3], ln_b[:], ALU.mult, ALU.add) \
                    .then_inc(ln_ok, 1)

            dve.wait_ge(*m.first_pass_done)
            for s in range(NS):
                add_y(0, s)
                dve.wait_ge(bank_free, s + 1)
                for j in range(NQ * s, NQ * (s + 1)):
                    add_x(0, j)
            dve.wait_ge(stage_used, x_item(0, KT - 1) + 1)
            add_pass(1)
            for k in range(KT - 1):
                split_y(k)
            add_pass(2)
            for s in range(NS):
                row_stats(s, range(NQ - 1))
            add_pass(3)
            dve.wait_ge(ln_in, 32)
            for s in range(NS + 1):
                if s < NS:
                    row_stats(s, [NQ - 1])
                    deviation(s)
                if s:
                    normalise(s - 1)
            add_pass(NQ)
            add_pass(NQ + 1)
            for j in range(KT):
                add_x(1, j)
            dve.wait_ge(stage_used, x_item(1, KT - 1) + 1)
            add_pass(NQ + 2)
            for s in range(NS):
                row_stats(s, range(NQ - 1))

            def scale_row(s):
                for h in range(2):
                    at = bass.ts(h, D_MODEL // 2)
                    dve.wait_ge(unit_ok, 2 * s + h + 1)
                    nc.vector.tensor_tensor(row[:, s, at], row[:, s, at], ln_g[:, at], ALU.mult).then_inc(scaled, 1)

            for s in range(NS):
                add_y(PASSES - 1, s)
                dve.wait_ge(bank_free, (PASSES - 1) * NS + s + 1)
                row_stats(s, [NQ - 1])
                deviation(s)
                one_over_root(1, s)
                nc.vector.scalar_tensor_tensor(dev[:, s, 3:4], mean_var[:, s, 0:1], -1.0, dev[:, s, 2:3], ALU.mult, ALU.mult) \
                    .then_inc(scale_ok, 1)
                if s:
                    scale_row(s - 1)
            scale_row(NS - 1)
            for h in range(2):
                at = bass.ts(h, D_MODEL // 2)
                dve.wait_ge(scaled, 2 * (NS - 1) + h + 1)
                nc.vector.tensor_tensor(row[:, NS - 1, at], row[:, NS - 1, at], ln_b[:, at], ALU.add).then_inc(last_ok, 1)


def hybrid_layer_kernel(nc, io):
    m = Mem()
    with ExitStack() as ctx, nc.Block() as block:
        def sem(name):
            return ctx.enter_context(nc.semaphore(name))
        top = Store(nc, ctx)
        m.x_hi = top.sb("x_hi", [P, KT, SEQ], F32R)[:]
        m.x_lo = top.sb("x_lo", [P, KT, SEQ], F32R)[:]
        until_out = ExitStack()
        st = Store(nc, until_out)
        m.ident = st.sb("ident", [P, P])[:]
        m.b_col = st.sb("b_col", [P, BIAS_COLS])[:]
        m.kw_bias = st.sb("kw_bias", [KW, 1])[:]
        m.rotary = st.sb("rotary", [P, 4])[:]
        tab_or_mask = st.sb("tab_or_mask", [P, max(2 * SEQ, MASK_COLS // 2)])[:]
        m.cos_i, m.sin_i = tab_or_mask[:, 0:SEQ], tab_or_mask[:, SEQ:2 * SEQ]
        m.mask = tab_or_mask[:, 0:MASK_COLS // 2].bitcast(BF16)
        with ExitStack() as until_picked:
            m.scores = Store(nc, until_picked).sb("scores", [P, SCORE_COLS])[:]
            load_index_phase(nc, block, sem, m, io)
            gate_phase(nc, block, sem, m, io)
        m.proj = [top.ps("proj0", [P, SEQ]), top.ps("proj1", [P, SEQ])]
        heads_phase(nc, block, sem, m, io)
        until_out.close()
        out_phase(nc, block, sem, m, io)


def rotary_constants():
    c = np.zeros((P, 4), np.float32)
    for n, dim in enumerate((D_IDX, HEAD_DIM)):
        inv = np.float32(ROPE_THETA) ** (-np.arange(0, dim, 2, dtype=np.float32) / np.float32(dim))
        c[:, n] = inv[np.arange(P) % (dim // 2)]
        c[:, 2 + n] = np.where(np.arange(P) % dim < dim // 2, -1, 1)
    return c


def kernel(x, p, positions, w_in, b_in, rel_bias, w_out, w_ple, w_ple_gate, b_ple_gate, ln_g, ln_b):
    import concourse.bacc as bacc
    from concourse.bass_utils import run_bass_kernel_spmd

    arrays = {
        "x": x.reshape(SEQ, D_MODEL), "p": p.reshape(SEQ, D_PLE), "positions": positions.reshape(SEQ),
        "w_in": w_in.reshape(D_MODEL, D_IN), "b_in": b_in.reshape(D_IN), "rel_bias": rel_bias.reshape(H_A, N_REL),
        "w_out": w_out.reshape(D_MODEL, D_MODEL), "w_ple": w_ple.reshape(D_PLE, D_MODEL),
        "w_pg": w_ple_gate.reshape(D_MODEL, D_MODEL), "b_pg": b_ple_gate.reshape(D_MODEL),
        "ln_g": ln_g.reshape(D_MODEL), "ln_b": ln_b.reshape(D_MODEL), "rotary": rotary_constants(),
    }
    nc = bacc.Bacc("TRN2", target_bir_lowering=False, num_devices=1)
    io, feeds = {}, {}
    for name, a in arrays.items():
        a = np.ascontiguousarray(a)
        feeds[f"in_{name}"] = a
        io[name] = nc.dram_tensor(f"in_{name}", a.shape, mybir.dt.from_np(a.dtype), kind="ExternalInput").ap()
    for name, shape in {"gate_term": (SEQ, D_MODEL), "rel_pad": (H_A, 3 * P), "rel_skew": (H_A, P, 2 * P),
                        "y": (H_A + H_B, HEAD_DIM, SEQ)}.items():
        io[name] = nc.dram_tensor(f"scratch_{name}", shape, F32, kind="Internal").ap()
    io["out"] = nc.dram_tensor("out_dram", (SEQ, D_MODEL), F32, kind="ExternalOutput").ap()
    hybrid_layer_kernel(nc, io)
    result = run_bass_kernel_spmd(nc, [feeds], core_ids=[0])
    return result.results[0]["out_dram"].reshape(x.shape)
```
